# Optimizing a Trainium2 kernel written in Bass

```python
import jax, jax.numpy as jnp
from jax import lax
import numpy as np
import math
import jax
import jax.numpy as jnp

D_MODEL = 1024
BATCH = 1
SEQ = 512
DEPTH = 4

N_MIXERS = 3
EPS = 1e-6
CHUNK = 128
A_WIDTH = 2 * D_MODEL
A_GROUPS = 8
A_GROUP_DIM = A_WIDTH // A_GROUPS
HEAD_DIM = 128
B_HEADS = D_MODEL // HEAD_DIM
B_PATTERNS = ((128, 1), (512, 4), (2048, 16))
N_B_GROUPS = len(B_PATTERNS)
B_WIDTH = B_HEADS * HEAD_DIM
B_IN_WIDTH = 3 * N_B_GROUPS * B_WIDTH + B_WIDTH
ROPE_DIM = HEAD_DIM // 4
ROPE_THETA = 500000.0
POOL_SIZES = (2, 4, 8, 16)
N_POOL = len(POOL_SIZES)
C_WIDTH = 2 * D_MODEL
C_GROUP = C_WIDTH // N_POOL
N_A = (DEPTH + 2) // 3
N_B = (DEPTH + 1) // 3
N_C = DEPTH // 3


def rms_norm(x, g):
    xf = x.astype(jnp.float32)
    y = xf * lax.rsqrt(jnp.mean(xf * xf, axis=-1, keepdims=True) + EPS)
    return (y * g.astype(jnp.float32)).astype(x.dtype)

def rotary_tables(seq_len):
    half = ROPE_DIM // 2
    inv_freq = jnp.power(jnp.float32(ROPE_THETA), -jnp.arange(half, dtype=jnp.float32) / half)
    ang = jnp.arange(seq_len, dtype=jnp.float32)[:, None] * inv_freq[None, :]
    return jnp.cos(ang)[None, :, None, :], jnp.sin(ang)[None, :, None, :]

def apply_partial_rotary(x, cos, sin):
    half = ROPE_DIM // 2
    x1 = x[..., :half].astype(jnp.float32)
    x2 = x[..., half:ROPE_DIM].astype(jnp.float32)
    rot = jnp.concatenate([x1 * cos - x2 * sin, x2 * cos + x1 * sin], axis=-1)
    return jnp.concatenate([rot.astype(x.dtype), x[..., ROPE_DIM:]], axis=-1)

def dilated_window_attention(q, k, v, span, dilation):
    bsz, S, H, hd = q.shape
    blk = span
    L = S // dilation
    nb = -(-L // blk)
    Lp = nb * blk

    def to_blocks(t):
        t = t.reshape(bsz, L, dilation, H, hd).transpose(0, 2, 1, 3, 4)
        t = jnp.pad(t, ((0, 0), (0, 0), (0, Lp - L), (0, 0), (0, 0)))
        return t.reshape(bsz, dilation, nb, blk, H, hd)

    def with_prev(t):
        prev = jnp.pad(t, ((0, 0), (0, 0), (1, 0), (0, 0), (0, 0), (0, 0)))[:, :, :-1]
        return jnp.concatenate([prev, t], axis=3)

    qb = to_blocks(q).astype(jnp.float32)
    kk = with_prev(to_blocks(k)).astype(jnp.float32)
    vv = with_prev(to_blocks(v)).astype(jnp.float32)
    scores = jnp.einsum('brnqhd,brnkhd->brnhqk', qb, kk) * (1.0 / np.sqrt(hd)).astype(np.float32)
    qi = jnp.arange(blk)[:, None]
    ki = jnp.arange(2 * blk)[None, :]
    dist = blk + qi - ki
    band = (dist >= 0) & (dist <= span)
    has_prev = (jnp.arange(nb) > 0)[:, None, None] | (ki >= blk)[None]
    mask = band[None] & has_prev
    scores = jnp.where(mask[None, None, :, None], scores, -jnp.inf)
    lse = jax.nn.logsumexp(scores, axis=-1)
    p = jnp.exp(scores - lse[..., None])
    o = jnp.einsum('brnhqk,brnkhd->brnqhd', p, vv)
    o = o.reshape(bsz, dilation, Lp, H, hd)[:, :, :L].transpose(0, 2, 1, 3, 4).reshape(bsz, S, H, hd)
    lse = lse.transpose(0, 1, 2, 4, 3).reshape(bsz, dilation, Lp, H)[:, :, :L]
    lse = lse.transpose(0, 2, 1, 3).reshape(bsz, S, H)
    return o, lse

def mixer_a(h, w_in, v_gain, w_s, b_s, w_out):
    bsz, S, _ = h.shape
    proj = h @ w_in
    u = proj[..., :A_WIDTH]
    v = rms_norm(proj[..., A_WIDTH:2 * A_WIDTH], v_gain)
    z = proj[..., 2 * A_WIDTH:]
    nc = S // CHUNK
    v = v.reshape(bsz, nc, CHUNK, A_GROUPS, A_GROUP_DIM)
    causal = jnp.tril(jnp.ones((CHUNK, CHUNK), dtype=bool))
    ws = jnp.where(causal[None], w_s, jnp.zeros_like(w_s))
    mixed = jnp.einsum('gij,bcjgd->bcigd', ws, v) + b_s.T[None, None, :, :, None]
    mixed = mixed.reshape(bsz, S, A_WIDTH)
    y = u * mixed * jax.nn.silu(z)
    return y @ w_out

def mixer_b(h, w_in, q_gain, k_gain, w_out):
    bsz, S, _ = h.shape
    proj = h @ w_in
    n_qkv = 3 * N_B_GROUPS * B_WIDTH
    qkv = proj[..., :n_qkv].reshape(bsz, S, 3, N_B_GROUPS, B_HEADS, HEAD_DIM)
    z = proj[..., n_qkv:]
    cos, sin = rotary_tables(S)
    outs, lses = [], []
    for g, (window, dilation) in enumerate(B_PATTERNS):
        q = apply_partial_rotary(rms_norm(qkv[:, :, 0, g], q_gain[g]), cos, sin)
        k = apply_partial_rotary(rms_norm(qkv[:, :, 1, g], k_gain[g]), cos, sin)
        o, lse = dilated_window_attention(q, k, qkv[:, :, 2, g], window // dilation, dilation)
        outs.append(o)
        lses.append(lse)
    wgt = jax.nn.softmax(jnp.stack(lses), axis=0)
    o = jnp.einsum('gbsh,gbshd->bshd', wgt, jnp.stack(outs))
    y = o.reshape(bsz, S, B_WIDTH).astype(h.dtype) * jax.nn.silu(z)
    return y @ w_out

def causal_mean(x, window):
    S = x.shape[1]
    c = jnp.cumsum(x.astype(jnp.float32), axis=1)
    c_prev = jnp.pad(c, ((0, 0), (window, 0), (0, 0)))[:, :S]
    cnt = jnp.minimum(jnp.arange(S) + 1, window).astype(jnp.float32)
    return ((c - c_prev) / cnt[None, :, None]).astype(x.dtype)

def mixer_c(h, w_in, w_grp, scale, w_out):
    bsz, S, _ = h.shape
    proj = h @ w_in
    xc = proj[..., :C_WIDTH].reshape(bsz, S, N_POOL, C_GROUP)
    z = proj[..., C_WIDTH:]
    pooled = jnp.stack([causal_mean(xc[:, :, g], w) for g, w in enumerate(POOL_SIZES)], axis=2)
    mixed = jnp.einsum('bsgc,gcd->bsgd', pooled - xc, w_grp).reshape(bsz, S, C_WIDTH) * scale
    y = mixed * jax.nn.silu(z)
    return y @ w_out

def first_inputs(seed: int = 0) -> dict:
    key = jax.random.key(seed)
    ks = jax.random.split(key, 16)
    f32 = jnp.float32

    def nrm(k, shape, fan_in):
        return jax.random.normal(k, shape, f32) * (fan_in ** -0.5)

    def gain(k, shape):
        return 1.0 + 0.1 * jax.random.normal(k, shape, f32)

    return {
        "x": jax.random.normal(ks[0], (BATCH, SEQ, D_MODEL), f32),
        "norm_gain": gain(ks[1], (DEPTH, D_MODEL)),
        "a_w_in": nrm(ks[2], (N_A, D_MODEL, 3 * A_WIDTH), D_MODEL),
        "a_v_gain": gain(ks[3], (N_A, A_WIDTH)),
        "a_w_s": nrm(ks[4], (N_A, A_GROUPS, CHUNK, CHUNK), CHUNK),
        "a_b_s": gain(ks[5], (N_A, A_GROUPS, CHUNK)),
        "a_w_out": nrm(ks[6], (N_A, A_WIDTH, D_MODEL), A_WIDTH),
        "b_w_in": nrm(ks[7], (N_B, D_MODEL, B_IN_WIDTH), D_MODEL),
        "b_q_gain": gain(ks[8], (N_B, N_B_GROUPS, HEAD_DIM)),
        "b_k_gain": gain(ks[9], (N_B, N_B_GROUPS, HEAD_DIM)),
        "b_w_out": nrm(ks[10], (N_B, B_WIDTH, D_MODEL), B_WIDTH),
        "c_w_in": nrm(ks[11], (N_C, D_MODEL, 2 * C_WIDTH), D_MODEL),
        "c_w_grp": nrm(ks[12], (N_C, N_POOL, C_GROUP, C_GROUP), C_GROUP),
        "c_scale": gain(ks[13], (N_C, C_WIDTH)),
        "c_w_out": nrm(ks[14], (N_C, C_WIDTH, D_MODEL), C_WIDTH),
    }

def first_block(x, norm_gain, a_w_in, a_v_gain, a_w_s, a_b_s, a_w_out,
              b_w_in, b_q_gain, b_k_gain, b_w_out,
              c_w_in, c_w_grp, c_scale, c_w_out):
    for i in range(DEPTH):
        kind, j = i % N_MIXERS, i // N_MIXERS
        h = rms_norm(x, norm_gain[i])
        if kind == 0:
            y = mixer_a(h, a_w_in[j], a_v_gain[j], a_w_s[j], a_b_s[j], a_w_out[j])
        elif kind == 1:
            y = mixer_b(h, b_w_in[j], b_q_gain[j], b_k_gain[j], b_w_out[j])
        else:
            y = mixer_c(h, c_w_in[j], c_w_grp[j], c_scale[j], c_w_out[j])
        x = x + y.astype(x.dtype)
    return x


DEPTH_2 = 2

GRID_W = 64
CTX_LEN = 256
N_LAYERS_A = (DEPTH_2 + 2) // N_MIXERS
N_LAYERS_B = (DEPTH_2 + 1) // N_MIXERS
N_LAYERS_C = DEPTH_2 // N_MIXERS
N_MOD = 6
HEAD_DIM_2 = 64
N_HEADS = D_MODEL // (2 * HEAD_DIM_2)
V_HEAD_DIM = 2 * HEAD_DIM_2
Q_BLOCK = 128
ROPE_THETA_2 = 10000.0
D_FF = 4 * D_MODEL
HYENA_EMB_DIM = 33
HYENA_FILTER_ORDER = 64
HYENA_SHORT_WIDTH = 3
HYENA_DECAY_TARGET = 1e-2
HYENA_FAST_DECAY_PCT = 0.3
HYENA_SLOW_DECAY_PCT = 1.5
CONV_WIDTH = 31
NORM_EPS = 1e-6
LN_EPS = 1e-5


def rms_norm_2(x, g, eps=NORM_EPS):
    xf = x.astype(jnp.float32)
    y = xf * lax.rsqrt(jnp.mean(xf * xf, axis=-1, keepdims=True) + eps)
    return (y * g.astype(jnp.float32)).astype(x.dtype)

def layer_norm(x, g, b, eps=LN_EPS):
    xf = x.astype(jnp.float32)
    mu = jnp.mean(xf, axis=-1, keepdims=True)
    var = jnp.mean(jnp.square(xf - mu), axis=-1, keepdims=True)
    y = (xf - mu) * lax.rsqrt(var + eps)
    return (y * g.astype(jnp.float32) + b.astype(jnp.float32)).astype(x.dtype)

def modulate(x, shift, scale):
    return x * (1.0 + scale) + shift

def depthwise_conv(x, w, b):
    y = lax.conv_general_dilated(
        x, w[:, None, :].astype(x.dtype), window_strides=(1,), padding="SAME",
        dimension_numbers=("NWC", "WIO", "NWC"), feature_group_count=x.shape[-1])
    return y + b

def grid_positions(n_tokens):
    rows = n_tokens // GRID_W
    row_ids = jnp.repeat(jnp.arange(rows, dtype=jnp.float32), GRID_W)
    col_ids = jnp.tile(jnp.arange(GRID_W, dtype=jnp.float32), rows)
    return row_ids, col_ids

def rope_1d(x, pos):
    half = x.shape[-1] // 2
    inv_freq = ROPE_THETA_2 ** (-jnp.arange(half, dtype=jnp.float32) / half)
    ang = pos[:, None] * inv_freq[None, :]
    cos = jnp.cos(ang)[None, :, None, :]
    sin = jnp.sin(ang)[None, :, None, :]
    x1 = x[..., :half].astype(jnp.float32)
    x2 = x[..., half:].astype(jnp.float32)
    return jnp.concatenate([x1 * cos - x2 * sin, x2 * cos + x1 * sin], axis=-1).astype(x.dtype)

def rope_2d(x, rows, cols):
    rd = x.shape[-1] // 2
    return jnp.concatenate([rope_1d(x[..., :rd], rows), rope_1d(x[..., rd:], cols)], axis=-1)

def diff_attend(q, k, v, lam):
    s = jnp.einsum("bqhpd,bkhpd->bhpqk", q, k).astype(jnp.float32) * (HEAD_DIM_2 ** -0.5)
    p = jax.nn.softmax(s, axis=-1)
    a = p[:, :, 0] - lam * p[:, :, 1]
    return jnp.einsum("bhqk,bkhe->bqhe", a.astype(v.dtype), v)

def differential_attention(u_lat, u_ctx, w_qkv, w_out, lam_vec, subln_g, lam_init, with_ctx):
    bsz, n_lat, _ = u_lat.shape

    def project(u):
        n = u.shape[1]
        q, k, v = jnp.split(u @ w_qkv, 3, axis=-1)
        return (q.reshape(bsz, n, N_HEADS, 2, HEAD_DIM_2),
                k.reshape(bsz, n, N_HEADS, 2, HEAD_DIM_2),
                v.reshape(bsz, n, N_HEADS, V_HEAD_DIM))

    q_l, k_l, v_l = project(u_lat)
    q_c, k_c, v_c = project(u_ctx)
    rows, cols = grid_positions(n_lat)
    q_l = rope_2d(q_l.reshape(bsz, n_lat, 2 * N_HEADS, HEAD_DIM_2), rows, cols).reshape(q_l.shape)
    k_l = rope_2d(k_l.reshape(bsz, n_lat, 2 * N_HEADS, HEAD_DIM_2), rows, cols).reshape(k_l.shape)
    lf = lam_vec.astype(jnp.float32)
    lam = jnp.exp(jnp.sum(lf[0] * lf[1])) - jnp.exp(jnp.sum(lf[2] * lf[3])) + lam_init
    k_all = jnp.concatenate([k_c, k_l], axis=1)
    v_all = jnp.concatenate([v_c, v_l], axis=1)
    n_blk = n_lat // Q_BLOCK
    q_blocks = jnp.moveaxis(q_l.reshape(bsz, n_blk, Q_BLOCK, N_HEADS, 2, HEAD_DIM_2), 1, 0)
    o_l = lax.map(lambda qb: diff_attend(qb, k_all, v_all, lam), q_blocks)
    o_l = jnp.moveaxis(o_l, 0, 1).reshape(bsz, n_lat, N_HEADS, V_HEAD_DIM)

    def merge_heads(o):
        o = rms_norm_2(o, subln_g) * (1.0 - lam_init)
        return o.reshape(bsz, o.shape[1], D_MODEL) @ w_out

    y_l = merge_heads(o_l)
    y_c = merge_heads(diff_attend(q_c, k_c, v_c, lam)) if with_ctx else None
    return y_l, y_c

def hyena_filters(n, w1, b1, w2, b2, freq, w_out):
    bands = (HYENA_EMB_DIM - 1) // 2
    t = jnp.linspace(0.0, 1.0, n, dtype=jnp.float32)[:, None]
    w = 2.0 * math.pi * jnp.arange(n, dtype=jnp.float32)[:, None] / n
    f = jnp.linspace(1e-4, bands - 1, bands, dtype=jnp.float32)[None, :]
    z = jnp.concatenate([t, jnp.cos(f * w), -jnp.sin(f * w)], axis=-1)
    hdn = jnp.sin(freq * (z @ w1 + b1))
    for j in range(w2.shape[0]):
        hdn = jnp.sin(freq * (hdn @ w2[j] + b2[j]))
    h = (hdn @ w_out).reshape(n, 2, D_MODEL)
    deltas = jnp.abs(jnp.linspace(math.log(HYENA_DECAY_TARGET) / HYENA_SLOW_DECAY_PCT,
                                  math.log(HYENA_DECAY_TARGET) / HYENA_FAST_DECAY_PCT,
                                  D_MODEL, dtype=jnp.float32))
    h = h * jnp.exp(-t * deltas[None, :])[:, None, :]
    return h[:, 0], h[:, 1]

def two_sided_fft_conv(v, h_fwd, h_bwd):
    n = v.shape[1]
    kern = jnp.concatenate([h_fwd, jnp.zeros((1, h_fwd.shape[1]), h_fwd.dtype), h_bwd[:0:-1]], axis=0)
    vf = jnp.fft.rfft(v.astype(jnp.float32), n=2 * n, axis=1)
    kf = jnp.fft.rfft(kern.astype(jnp.float32), n=2 * n, axis=0)
    y = jnp.fft.irfft(vf * kf[None], n=2 * n, axis=1)[:, :n]
    return y.astype(v.dtype)

def hyena_mixer(u, w_in, b_in, w_short, b_short, fw1, fb1, fw2, fb2, ffreq, fw_out, d_bias, w_out, b_out):
    z = depthwise_conv(u @ w_in + b_in, w_short, b_short)
    x0, x1, v = jnp.split(z, 3, axis=-1)
    h_fwd, h_bwd = hyena_filters(u.shape[1], fw1, fb1, fw2, fb2, ffreq, fw_out)
    v = v * x1
    v = two_sided_fft_conv(v, h_fwd, h_bwd) + v * d_bias
    return (v * x0) @ w_out + b_out

def conformer_conv(u, w_pw1, b_pw1, w_dw, b_dw, ln_g, ln_b, w_pw2, b_pw2):
    a, g = jnp.split(u @ w_pw1 + b_pw1, 2, axis=-1)
    z = depthwise_conv(a * jax.nn.sigmoid(g), w_dw, b_dw)
    z = jax.nn.silu(layer_norm(z, ln_g, ln_b))
    return z @ w_pw2 + b_pw2

def squared_relu_mlp(u, w_in, w_out):
    return jnp.square(jax.nn.relu(u @ w_in)) @ w_out

def second_inputs(seed: int = 0) -> dict:
    key = jax.random.key(seed)
    ks = iter(jax.random.split(key, 48))
    D = D_MODEL

    def nrm(shape, scale):
        return scale * jax.random.normal(next(ks), shape, jnp.float32)

    return {
        "x": nrm((BATCH, SEQ, D), 1.0),
        "c": nrm((BATCH, D), 1.0),
        "ctx": nrm((BATCH, CTX_LEN, D), 1.0),
        "c_ctx": nrm((D,), 1.0),
        "w_mod": nrm((DEPTH_2, D, N_MOD * D), 0.5 * D ** -0.5),
        "b_mod": nrm((DEPTH_2, N_MOD * D), 0.02),
        "norm_mix_pre": 1.0 + nrm((DEPTH_2, D), 0.05),
        "norm_mix_post": 1.0 + nrm((DEPTH_2, D), 0.05),
        "norm_mlp_pre": 1.0 + nrm((DEPTH_2, D), 0.05),
        "norm_mlp_post": 1.0 + nrm((DEPTH_2, D), 0.05),
        "w_mlp_in": nrm((DEPTH_2, D, D_FF), D ** -0.5),
        "w_mlp_out": nrm((DEPTH_2, D_FF, D), D_FF ** -0.5),
        "attn_w_qkv": nrm((N_LAYERS_A, D, 3 * D), D ** -0.5),
        "attn_w_out": nrm((N_LAYERS_A, D, D), D ** -0.5),
        "attn_lambda": nrm((N_LAYERS_A, 4, HEAD_DIM_2), 0.1),
        "attn_subln": 1.0 + nrm((N_LAYERS_A, V_HEAD_DIM), 0.05),
        "hy_w_in": nrm((N_LAYERS_B, D, 3 * D), D ** -0.5),
        "hy_b_in": nrm((N_LAYERS_B, 3 * D), 0.02),
        "hy_w_short": nrm((N_LAYERS_B, HYENA_SHORT_WIDTH, 3 * D), HYENA_SHORT_WIDTH ** -0.5),
        "hy_b_short": nrm((N_LAYERS_B, 3 * D), 0.02),
        "hy_filt_w1": nrm((N_LAYERS_B, HYENA_EMB_DIM, HYENA_FILTER_ORDER), HYENA_EMB_DIM ** -0.5),
        "hy_filt_b1": nrm((N_LAYERS_B, HYENA_FILTER_ORDER), 0.1),
        "hy_filt_w2": nrm((N_LAYERS_B, 2, HYENA_FILTER_ORDER, HYENA_FILTER_ORDER), HYENA_FILTER_ORDER ** -0.5),
        "hy_filt_b2": nrm((N_LAYERS_B, 2, HYENA_FILTER_ORDER), 0.1),
        "hy_filt_freq": 1.0 + nrm((N_LAYERS_B, HYENA_FILTER_ORDER), 0.05),
        "hy_filt_w_out": nrm((N_LAYERS_B, HYENA_FILTER_ORDER, 2 * D), HYENA_FILTER_ORDER ** -0.5),
        "hy_bias": nrm((N_LAYERS_B, D), 1.0),
        "hy_w_out": nrm((N_LAYERS_B, D, D), D ** -0.5),
        "hy_b_out": nrm((N_LAYERS_B, D), 0.02),
        "cv_w_pw1": nrm((N_LAYERS_C, D, 2 * D), D ** -0.5),
        "cv_b_pw1": nrm((N_LAYERS_C, 2 * D), 0.02),
        "cv_w_dw": nrm((N_LAYERS_C, CONV_WIDTH, D), CONV_WIDTH ** -0.5),
        "cv_b_dw": nrm((N_LAYERS_C, D), 0.02),
        "cv_ln_g": 1.0 + nrm((N_LAYERS_C, D), 0.05),
        "cv_ln_b": nrm((N_LAYERS_C, D), 0.02),
        "cv_w_pw2": nrm((N_LAYERS_C, D, D), D ** -0.5),
        "cv_b_pw2": nrm((N_LAYERS_C, D), 0.02),
    }

def second_block(x, c, ctx, c_ctx, w_mod, b_mod, norm_mix_pre, norm_mix_post, norm_mlp_pre, norm_mlp_post,
              w_mlp_in, w_mlp_out, attn_w_qkv, attn_w_out, attn_lambda, attn_subln,
              hy_w_in, hy_b_in, hy_w_short, hy_b_short, hy_filt_w1, hy_filt_b1, hy_filt_w2, hy_filt_b2,
              hy_filt_freq, hy_filt_w_out, hy_bias, hy_w_out, hy_b_out,
              cv_w_pw1, cv_b_pw1, cv_w_dw, cv_b_dw, cv_ln_g, cv_ln_b, cv_w_pw2, cv_b_pw2):
    h_lat, h_ctx = x, ctx
    silu_c = jax.nn.silu(c)
    silu_cc = jax.nn.silu(c_ctx)
    for i in range(DEPTH_2):
        last = i == DEPTH_2 - 1
        kind, j = i % N_MIXERS, i // N_MIXERS
        need_ctx_out = not last
        need_ctx_in = need_ctx_out or kind == 0
        mod_l = jnp.split((silu_c @ w_mod[i] + b_mod[i])[:, None, :], N_MOD, axis=-1)
        mod_c = jnp.split(silu_cc @ w_mod[i] + b_mod[i], N_MOD, axis=-1)
        u_l = modulate(rms_norm_2(h_lat, norm_mix_pre[i]), mod_l[0], mod_l[1])
        u_c = modulate(rms_norm_2(h_ctx, norm_mix_pre[i]), mod_c[0], mod_c[1]) if need_ctx_in else None
        if kind == 0:
            y_l, y_c = differential_attention(u_l, u_c, attn_w_qkv[j], attn_w_out[j], attn_lambda[j],
                                              attn_subln[j], 0.8 - 0.6 * math.exp(-0.3 * i), need_ctx_out)
        elif kind == 1:
            hp = (hy_w_in[j], hy_b_in[j], hy_w_short[j], hy_b_short[j], hy_filt_w1[j], hy_filt_b1[j],
                  hy_filt_w2[j], hy_filt_b2[j], hy_filt_freq[j], hy_filt_w_out[j], hy_bias[j],
                  hy_w_out[j], hy_b_out[j])
            y_l = hyena_mixer(u_l, *hp)
            y_c = hyena_mixer(u_c, *hp) if need_ctx_out else None
        else:
            cp = (cv_w_pw1[j], cv_b_pw1[j], cv_w_dw[j], cv_b_dw[j], cv_ln_g[j], cv_ln_b[j],
                  cv_w_pw2[j], cv_b_pw2[j])
            y_l = conformer_conv(u_l, *cp)
            y_c = conformer_conv(u_c, *cp) if need_ctx_out else None
        h_lat = h_lat + mod_l[2] * rms_norm_2(y_l, norm_mix_post[i])
        v_l = modulate(rms_norm_2(h_lat, norm_mlp_pre[i]), mod_l[3], mod_l[4])
        h_lat = h_lat + mod_l[5] * rms_norm_2(squared_relu_mlp(v_l, w_mlp_in[i], w_mlp_out[i]), norm_mlp_post[i])
        if need_ctx_out:
            h_ctx = h_ctx + mod_c[2] * rms_norm_2(y_c, norm_mix_post[i])
            v_c = modulate(rms_norm_2(h_ctx, norm_mlp_pre[i]), mod_c[3], mod_c[4])
            h_ctx = h_ctx + mod_c[5] * rms_norm_2(squared_relu_mlp(v_c, w_mlp_in[i], w_mlp_out[i]), norm_mlp_post[i])
    return h_lat


def setup_inputs(seed=0):
    out = dict(first_inputs(seed))
    for name, value in second_inputs(seed + 1).items():
        if name != "x":
            out[name + "_2"] = value
    return out


def reference(
    x, norm_gain, a_w_in, a_v_gain, a_w_s, a_b_s, a_w_out, b_w_in, b_q_gain, b_k_gain, b_w_out,
    c_w_in, c_w_grp, c_scale, c_w_out, c_2, ctx_2, c_ctx_2, w_mod_2, b_mod_2, norm_mix_pre_2,
    norm_mix_post_2, norm_mlp_pre_2, norm_mlp_post_2, w_mlp_in_2, w_mlp_out_2, attn_w_qkv_2,
    attn_w_out_2, attn_lambda_2, attn_subln_2, hy_w_in_2, hy_b_in_2, hy_w_short_2, hy_b_short_2,
    hy_filt_w1_2, hy_filt_b1_2, hy_filt_w2_2, hy_filt_b2_2, hy_filt_freq_2, hy_filt_w_out_2,
    hy_bias_2, hy_w_out_2, hy_b_out_2, cv_w_pw1_2, cv_b_pw1_2, cv_w_dw_2, cv_b_dw_2, cv_ln_g_2,
    cv_ln_b_2, cv_w_pw2_2, cv_b_pw2_2,
):
    x = first_block(
        x, norm_gain, a_w_in, a_v_gain, a_w_s, a_b_s, a_w_out, b_w_in, b_q_gain, b_k_gain,
        b_w_out, c_w_in, c_w_grp, c_scale, c_w_out,
    )
    return second_block(
        x, c_2, ctx_2, c_ctx_2, w_mod_2, b_mod_2, norm_mix_pre_2, norm_mix_post_2,
        norm_mlp_pre_2, norm_mlp_post_2, w_mlp_in_2, w_mlp_out_2, attn_w_qkv_2, attn_w_out_2,
        attn_lambda_2, attn_subln_2, hy_w_in_2, hy_b_in_2, hy_w_short_2, hy_b_short_2,
        hy_filt_w1_2, hy_filt_b1_2, hy_filt_w2_2, hy_filt_b2_2, hy_filt_freq_2, hy_filt_w_out_2,
        hy_bias_2, hy_w_out_2, hy_b_out_2, cv_w_pw1_2, cv_b_pw1_2, cv_w_dw_2, cv_b_dw_2,
        cv_ln_g_2, cv_ln_b_2, cv_w_pw2_2, cv_b_pw2_2,
    )


_drawn_inputs = setup_inputs


def setup_inputs(seed=0):
    import zlib

    import numpy as np

    out = dict(_drawn_inputs(seed))
    spreads = {}
    factors = {'b_q_gain': 7.577,
     'b_k_gain': 6.677,
     'norm_mix_pre_2': 3.272,
     'norm_mix_post_2': 4.014,
     'norm_mlp_pre_2': 3.641,
     'norm_mlp_post_2': 4.183,
     'attn_lambda_2': 8.0,
     'attn_subln_2': 7.015,
     'hy_b_in_2': 5.621,
     'hy_b_short_2': 6.767,
     'hy_filt_freq_2': 5.085,
     'hy_b_out_2': 8.0}
    for name, (base, spread) in spreads.items():
        noise = np.random.default_rng([zlib.crc32(name.encode()), seed]).standard_normal(out[name].shape)
        drawn = base * np.exp(spread * noise) if base else spread * noise
        out[name] = jnp.asarray(drawn.astype(out[name].dtype))
    for name, factor in factors.items():
        out[name] = (out[name] * factor).astype(out[name].dtype)
    return out
```

```python
from contextlib import ExitStack

import numpy as np

import concourse.bass as bass
from concourse import mybir

F32 = mybir.dt.float32
F32R = mybir.dt.float32r
BF16 = mybir.dt.bfloat16
ALU = mybir.AluOpType
ACT = mybir.ActivationFunctionType
AX = mybir.AxisListType

P = 128
S = 512
D = 1024
KD = D // P
TT = S // P
CTX = 256
CT = CTX // P
AW = 2 * D
DFF = 4 * D
NEG = -1e30
EPS = 1e-6
LAM_INIT = 0.8 - 0.6 * float(np.exp(-0.3 * 0))
CREDIT = 4096


class Mark:

    def __init__(self, ctr, const, levels, back=0):
        self.ctr, self.const, self.levels, self.back = ctr, const, levels, back


class Counter:
    def __init__(self, sem, step, start=0):
        self.sem, self.step, self.const = sem, step, start


class Loop:
    def __init__(self, i, n, per, start, table):
        self.i, self.n, self.per, self.start, self.table = i, n, per, start, table
        self.seen = set()


class Program:

    def __init__(self, nc, sem):
        self.nc, self.sem = nc, sem
        self.eng = {"pe": nc.tensor, "act": nc.scalar, "dve": nc.vector, "pool": nc.gpsimd, "sp": nc.sync}
        self.ctr = {}
        for n in ("pe", "act", "dve", "pool"):
            self.ctr[n] = Counter(sem("done_" + n), 1, CREDIT)
        self.pins = sem("pins")
        self.loops = []
        self.names = {}
        self.dry = 0
        self.drytab = None

    def credit(self):
        for n in ("pe", "act", "dve", "pool"):
            self.eng[n].sem_inc(self.ctr[n].sem, CREDIT)

    def dma_counter(self, name):
        self.ctr[name] = Counter(self.sem(name), 16)
        return name

    def emit(self, e, fn, ctr=None, name=None):
        c = self.ctr[ctr or e]
        if not self.dry:
            fn(self.eng[e]).then_inc(c.sem, c.step)
        c.const += c.step
        m = Mark(c, c.const, tuple(self.loops))
        if name:
            self.name(name, m)
        return m

    def raw(self, e, fn):
        if not self.dry:
            fn(self.eng[e])

    def name(self, name, m):
        self.names[name] = m
        if self.dry and self.drytab is not None:
            self.drytab[name] = (m.ctr, m.const - self.drystart[m.ctr])
        elif self.loops:
            self.loops[-1].seen.add(name)

    def last(self, name):
        if self.dry:
            return self.names.get(name)
        if self.loops:
            lp = self.loops[-1]
            if name not in lp.seen and name in lp.table:
                ctr, rel = lp.table[name]
                return Mark(ctr, lp.start[ctr] + rel, tuple(self.loops), back=lp.per[ctr])
        return self.names.get(name)

    def value(self, m):
        v = m.const - m.back
        out = None
        for lp in m.levels:
            per = lp.per[m.ctr]
            if lp in self.loops:
                if per:
                    term = lp.i * per
                    out = term if out is None else out + term
            else:
                v += per * (lp.n - 1)
        return v if out is None else out + v

    def wait(self, e, *marks):
        if self.dry:
            return
        for m in marks:
            if isinstance(m, str):
                m = self.last(m)
            if m is not None:
                self.eng[e].wait_ge(m.ctr.sem, self.value(m))

    def loop(self, n, body, carry=()):
        for e, *names in carry:
            self.wait(e, *[x for x in names if x in self.names])
            if self.loops:
                self.pin(e)
        ctrs = list(self.ctr.values())
        saved_names, saved_tab, saved_start = dict(self.names), self.drytab, (self.drystart if self.dry else None)
        start = {c: c.const for c in ctrs}
        self.dry += 1
        self.drytab, self.drystart = {}, start
        body(0)
        table = self.drytab
        per = {c: c.const - start[c] for c in ctrs}
        self.dry -= 1
        self.drytab, self.drystart = saved_tab, saved_start
        if self.dry:
            for c in ctrs:
                c.const = start[c] + per[c] * n
            for k, (c, rel) in table.items():
                self.drytab[k] = (c, start[c] + per[c] * (n - 1) + rel - self.drystart[c])
            return
        for c in ctrs:
            c.const = start[c]
        self.names = saved_names
        with self.nc.Fori(0, n) as i:
            self.loops.append(Loop(i, n, per, start, table))
            body(i)
            self.loops.pop()
        for c in ctrs:
            c.const = start[c] + per[c] * n
        if self.loops:
            self.loops[-1].seen.update(table)

    def A(self, fn, *waits, name=None):
        self.wait("act", *waits)
        return self.emit("act", fn, name=name)

    def pin(self, e):
        if not self.dry:
            self.eng[e].sem_inc(self.pins, 1)

    def Adyn(self, fn, *waits, name=None):
        self.wait("act", *waits)
        self.pin("act")
        return self.emit("act", fn, name=name)

    def Vpin(self, fn, *waits, name=None):
        self.wait("dve", *waits)
        self.pin("dve")
        return self.emit("dve", fn, name=name)

    def V(self, fn, *waits, name=None):
        self.wait("dve", *waits)
        return self.emit("dve", fn, name=name)

    def G(self, fn, *waits, name=None):
        self.wait("pool", *waits)
        return self.emit("pool", fn, name=name)

    def T(self, fn, *waits, name=None):
        self.wait("pe", *waits)
        return self.emit("pe", fn, name=name)


PACKS = [
    [("norm_gain", 4 * KD), ("a_v_gain", 2 * AW // P), ("c_scale", AW // P), ("b_q_gain", 3), ("b_k_gain", 3),
     ("c_2", KD), ("c_ctx_2", KD)],
    [("norm_mix_pre_2", 2 * KD), ("norm_mix_post_2", 2 * KD), ("norm_mlp_pre_2", 2 * KD), ("norm_mlp_post_2", 2 * KD),
     ("attn_subln_2", 1), ("hy_b_in_2", 3 * KD), ("hy_b_short_2", 3 * KD), ("hy_bias_2", KD)],
    [("hy_w_short_2", 9 * KD), ("hy_b_out_2", KD)],
    [("b_mod_2", 12 * KD)],
]


def flat_rows(ap):
    shape = ap.shape
    if len(shape) == 1:
        return ap.rearrange("(r p) -> r p", p=P)
    if len(shape) == 2:
        return ap.rearrange("a (r p) -> (a r) p", p=P)
    return ap.rearrange("a b (r p) -> (a b r) p", p=P)


def build(nc, I, out):
    ctx = ExitStack()
    with ctx:
        def sem(name):
            return ctx.enter_context(nc.semaphore(name))

        def sb(name, shape, dt=F32, st=ctx):
            return st.enter_context(nc.sbuf_tensor(name, shape, dt))

        pr = Program(nc, sem)
        A, Ad, V, Vp, G, T = pr.A, pr.Adyn, pr.V, pr.Vpin, pr.G, pr.T

        x = sb("x", [P, KD, S])
        Yh, Yl = sb("Yh", [P, KD, S], F32R), sb("Yl", [P, KD, S], F32R)
        Wr = sb("Wr", [P, 2, 2048])
        Wh, Wl = sb("Wh", [P, 2, 2048], F32R), sb("Wl", [P, 2, 2048], F32R)
        ones, ident = sb("ones", [P, P]), sb("ident", [P, P])
        NCOL = sum(r for pk in PACKS for _, r in pk)
        PK = sb("PK", [P, NCOL])
        mod = sb("mod", [P, 96, 2])
        GC = sb("GC", [P, 2, 5, KD])
        sc2 = sb("sc2", [P, KD, 2])
        eps = sb("eps", [P, 2])
        acc = sb("acc", [P, S])
        rs = sb("rs", [P, 2, S])
        sq = sb("sq", [P, 2, S])
        tmp = sb("tmp", [P, 4, S])
        ps = [ctx.enter_context(nc.psum_tensor(f"ps{b}", [P, S], F32)) for b in range(4)]
        psx = ctx.enter_context(nc.psum_tensor("psx", [P, 4, S], F32))
        kspec = nc.dram_tensor("kspec", (2, TT, P, D), F32).ap()

        col = {}
        off = 0
        for pk in PACKS:
            for n, r in pk:
                col[n] = off
                off += r

        def pc(name, i):
            return PK[:, col[name] + i:col[name] + i + 1]

        def phase(*tensors):
            with ExitStack() as st:
                return [sb(n, s, d, st) for n, s, d in tensors]

        with ExitStack() as over:
            Ah, Al = sb("Ah", [P, KD, S], F32R, over), sb("Al", [P, KD, S], F32R, over)
            stage, rows = phase(("stage", [P, TT, D], F32), ("rows", [P, 4, P], F32))
            vA, wsT, bA, szA, modw, ssA, vst = phase(
                ("vA", [P, TT, AW], F32), ("wsT", [P, 8, P], F32), ("bA", [P, 8, P], F32), ("szA", [P, 2, S], F32),
                ("modw", [P, 2, KD, P], F32), ("ssA", [P, 16], F32), ("vst", [P, 2, S], F32))
            QB, KB, VB, maskB, PB, ropeB, onB, stB = phase(
                ("QB", [P, 3, 2, S], F32), ("KB", [P, 3, 2, S], F32), ("VB", [P, 3, TT, 256], F32),
                ("maskB", [P, 27 * P], BF16), ("PB", [P, 2304], F32), ("ropeB", [32, 2, S], F32), ("onB", [P, P], F32),
                ("stB", [P, 2, 4], F32))
            xcC, s0C, s1C, Ch, Cl, szC, cntC = phase(
                ("xcC", [P, 2, S + 16], F32), ("s0C", [P, S + 16], F32), ("s1C", [P, S + 16], F32),
                ("Ch", [P, 4, S], F32R), ("Cl", [P, 4, S], F32R), ("szC", [P, 4, S], F32), ("cntC", [P, 4, S], F32))
            QD, KDt, VD, Uh, Ul, PD, ropeD, stD = phase(
                ("QD", [P, 4, S], F32), ("KDt", [P, 4, S + CTX], F32), ("VD", [P, TT + CT, 512], F32),
                ("Uh", [P, KD, CTX], F32R), ("Ul", [P, KD, CTX], F32R), ("PD", [P, 2, S + CTX], F32),
                ("ropeD", [P, 2, S], F32), ("stD", [P, 24], F32))
            yt, = phase(("yt", [P, KD, S], F32))
            x0H, wH, uH = phase(("x0H", [P, KD, S], F32), ("wH", [P, KD, S], F32), ("uH", [P, 2, S + 2], F32))
            zF, hdF, w1F, w2F, woF, colF, kF, tabF, hsF, hdiffF, dlF, kcF = phase(
                ("zF", [33, S], F32), ("hdF", [64, 2, S], F32), ("w1F", [33, 64], F32), ("w2F", [64, 2, 64], F32),
                ("woF", [64, 2 * D], F32), ("colF", [P, 16], F32), ("kF", [64, S], F32), ("tabF", [P, 2, TT, S], F32),
                ("hsF", [P, TT, 512], F32), ("hdiffF", [P, TT, 512], F32), ("dlF", [P, D], F32), ("kcF", [P, 2, 512], F32))
        kS, yS, over0, tabH, wtH = phase(
            ("kS", [P, 2, TT, 512], F32), ("yS", [P, 2, TT, 512], F32), ("over0", [P, 2 * KD, S], F32),
            ("tabH", [P, 2, TT, 512], F32), ("wtH", [P, TT, 512], F32))

        block = ctx.enter_context(nc.Block())
        pr.credit()

        raw = [pr.dma_counter("raw0"), pr.dma_counter("raw1")]
        pr.ctr["hi"] = Counter(sem("hi"), 1, CREDIT)
        pr.ctr["lo"] = Counter(sem("lo"), 1, CREDIT)
        pr.ctr["panels"] = Counter(None, 1, CREDIT)
        nc.scalar.sem_inc(pr.ctr["hi"].sem, CREDIT)
        nc.gpsimd.sem_inc(pr.ctr["lo"].sem, CREDIT)
        state = {"n": 0}

        def split_done(behind):
            c = pr.ctr["panels"]
            return Mark(pr.ctr["lo"], c.const, tuple(pr.loops), back=behind)

        def load_panel(src):
            s = state["n"] % 2
            state["n"] += 1
            pr.wait("sp", split_done(1))
            pr.pin("sp")
            pr.emit("sp", lambda e: e.dma_start(Wr[:, s, :].rearrange("p (k n) -> p k n", k=src.shape[1]), src), ctr=raw[s])
            pr.ctr["panels"].const += 1
            return s

        def split_panel(s):
            c = pr.ctr[raw[s]]
            pr.wait("act", Mark(c, c.const, tuple(pr.loops), back=-16), "pe_slot%d" % s)
            mh = pr.emit("act", lambda e: e.activation(Wh[:, s, :], Wr[:, s, :], ACT.Copy), ctr="hi")
            pr.wait("pool", mh)
            pr.emit("pool", lambda e: e.tensor_tensor(Wl[:, s, :], Wr[:, s, :], Wh[:, s, :].bitcast(F32), ALU.subtract), ctr="lo")

        def panel(src, tiles, epis, more=True):
            s = load_panel(src)
            if more:
                split_panel(1 - s)
            pr.wait("pe", split_done(0))
            for n, (tile, epi) in enumerate(zip(tiles, epis)):
                m = tile(s)
                if n == len(tiles) - 1:
                    pr.name("pe_slot%d" % s, m)
                epi(m)

        def mm3(o, ah, al, bh, bl, first, last):
            pr.raw("pe", lambda e: e.matmul(o, ah, bh, start=first, stop=False))
            pr.raw("pe", lambda e: e.matmul(o, ah, bl, start=False, stop=False))
            return lambda e: e.matmul(o, al, bh, start=False, stop=last)

        def wpart(W, s, k, c0, c1, kt=KD):
            return W[:, s, :].rearrange("p (k n) -> p k n", k=kt)[:, k, c0:c1]

        def tile_F(n, hi, lo, bank, ready=None, kt=KD, cols=S, width=None):
            def go(s):
                pr.wait("pe", "rel%d" % bank)
                m = None
                for k in range(kt):
                    if ready:
                        pr.wait("pe", ready(k))
                    f = mm3(ps[bank][:, 0:cols], wpart(Wh, s, k, n * P, n * P + P, kt), wpart(Wl, s, k, n * P, n * P + P, kt),
                            hi[:, k, :], lo[:, k, :], k == 0, k == kt - 1)
                    if k < kt - 1:
                        pr.raw("pe", f)
                    else:
                        m = pr.emit("pe", f)
                return m
            return go

        def tile_T(pair, hi, lo, bank, ready=None):
            def go(s):
                pr.wait("pe", "rel%d" % bank)
                m = None
                for j, t in enumerate(pair):
                    for k in range(KD):
                        if ready:
                            pr.wait("pe", ready(k))
                        f = mm3(ps[bank][:, j * 256:(j + 1) * 256], hi[:, k, t * P:(t + 1) * P], lo[:, k, t * P:(t + 1) * P],
                                wpart(Wh, s, k, 0, 256), wpart(Wl, s, k, 0, 256), k == 0, k == KD - 1)
                        if k < KD - 1 or t != pair[-1]:
                            pr.raw("pe", f)
                        else:
                            m = pr.emit("pe", f)
                return m
            return go

        CARRY = [("pe", "rel0", "rel1", "rel2", "rel3"), ("act", "pe_slot0", "pe_slot1")]

        def ksrc(w, k0, n0):
            return w.rearrange("(k p) n -> p k n", p=P)[:, bass.ds(k0, KD), bass.ds(n0, 256)]

        def now(e):
            c = pr.ctr[e]
            return Mark(c, c.const, tuple(pr.loops))

        def new_phase(*more):
            for e in ("act", "dve", "pe", "pool") + more:
                pr.wait(e, now("act"), now("dve"), now("pe"), now("pool"))

        pr.dma_counter("ldc")
        pr.dma_counter("ldx")
        ml = None
        for b in range(TT):
            ml = pr.emit("sp", lambda e: e.dma_start(stage[:, b, :], I["x"][0, b * P:(b + 1) * P, :]), ctr="ldx")
        m_x = ml
        pr.emit("act", lambda e: e.dma_start(ident[:], I["k_ident"]), ctr="ldc")
        for n, pk in enumerate(PACKS):
            r = 0
            for name, cnt in pk:
                ml = pr.emit("act", lambda e: e.dma_start(rows[r:r + cnt, n, :], flat_rows(I[name])), ctr="ldc")
                r += cnt
        m_c = ml
        V(lambda e: e.memset(ones[:], 1.0), name="ones")
        V(lambda e: e.memset(eps[:], EPS))
        m_one = V(lambda e: e.memset(acc[:], 0.0), name="acc")
        pr.wait("pe", m_c)
        off = 0
        for n, pk in enumerate(PACKS):
            r = sum(c for _, c in pk)
            m = T(lambda e: e.transpose(psx[:, 0, off:off + r], rows[0:r, n, :], ident[0:r, 0:r]))
            off += r
        m = V(lambda e: e.tensor_copy(PK[:], psx[:, 0, 0:NCOL]), m, name="PK")
        pr.name("relx0", m)
        pr.wait("pe", m_x)
        for k in range(KD):
            b = k % 4
            pr.wait("pe", "rel%d" % b)
            for t in range(TT):
                m = T(lambda e: e.transpose(ps[b][:, t * P:(t + 1) * P], stage[:, t, k * P:(k + 1) * P], ident[:]))
            mx = V(lambda e: e.tensor_copy(x[:, k, :], ps[b][:]), m, name="rel%d" % b)
            ms = A(lambda e: e.activation(sq[:, k % 2, :], x[:, k, :], ACT.Square), mx, "sqr%d" % (k % 2))
            m_one = V(lambda e: e.tensor_tensor(acc[:], acc[:], sq[:, k % 2, :], ALU.add), ms, m_one, name="sqr%d" % (k % 2))
        pr.name("acc", m_one)
        m = A(lambda e: e.activation(sc2[:, :, 0], PK[:, col["c_2"]:col["c_2"] + KD], ACT.Silu), "PK")
        m_sc = A(lambda e: e.activation(sc2[:, :, 1], PK[:, col["c_ctx_2"]:col["c_ctx_2"] + KD], ACT.Silu), name="sc2")

        def rstd(src_marks, width, n_feat, r=0, bank=3, src=None, cols=S):
            m = T(lambda e: e.matmul(psx[:, bank, 0:cols], ones[:], src, start=True, stop=True),
                  src_marks, "ones", "relx%d" % bank)
            m = A(lambda e: e.activation(rs[:, r, 0:cols], psx[:, bank, 0:cols], ACT.Sqrt, bias=eps[:, 0:1], scale=1.0 / n_feat),
                  m, "rsr%d" % r, name="relx%d" % bank)
            return V(lambda e: e.reciprocal(rs[:, r, 0:cols], rs[:, r, 0:cols]), m)

        def norm(gain, bias=None, srcx=x, hi=Ah, lo=Al, free="pe_all", cols=S, tag="h"):
            m = rstd("acc", S, D, src=acc[:, 0:cols], cols=cols)
            pr.wait("act", free)
            pr.wait("dve", free)
            pend = []

            def fin(k, mh):
                V(lambda e: e.tensor_tensor(lo[:, k, :], tmp[:, k % 4, 0:cols], hi[:, k, :].bitcast(F32), ALU.subtract),
                  mh, name="%s%d" % (tag, k))
                pr.name("tmp%d" % (k % 4), pr.names["%s%d" % (tag, k)])
            for k in range(KD):
                mt = V(lambda e: e.scalar_tensor_tensor(tmp[:, k % 4, 0:cols], srcx[:, k, :], gain(k), rs[:, 0, 0:cols],
                                                        ALU.mult, ALU.mult), m, "tmp%d" % (k % 4))
                if k == KD - 1:
                    pr.name("rsr0", mt)
                if bias:
                    mt = V(lambda e: e.tensor_scalar(tmp[:, k % 4, 0:cols], tmp[:, k % 4, 0:cols], bias(k), None, ALU.add), mt)
                mh = A(lambda e: e.activation(hi[:, k, :], tmp[:, k % 4, 0:cols], ACT.Copy), mt)
                pend.append((k, mh))
                if len(pend) > 1:
                    fin(*pend.pop(0))
            while pend:
                fin(*pend.pop(0))

        def y_ready(k):
            return "y%d" % k

        def h_ready(k):
            return "h%d" % k

        def out_product(w, k0, final, hi=Yh, lo=Yl, last_panels=False):
            if final:
                m0 = V(lambda e: e.memset(acc[:], 0.0), "acc_read", name="accw")

            def body(i, last=False):
                def epi(b):
                    def go(m):
                        n = i * 4 + b
                        mx = V(lambda e: e.tensor_tensor(x[:, bass.ds(n, 1), :], x[:, bass.ds(n, 1), :],
                                                         ps[b][:].rearrange("p (a n) -> p a n", a=1), ALU.add),
                               m, name="rel%d" % b)
                        if final:
                            ms = Ad(lambda e: e.activation(sq[:, b % 2, :].rearrange("p (a n) -> p a n", a=1),
                                                           x[:, bass.ds(n, 1), :], ACT.Square), mx, "sqr%d" % (b % 2))
                            V(lambda e: e.tensor_tensor(acc[:], acc[:], sq[:, b % 2, :], ALU.add), ms, "accw", name="accw")
                            pr.name("sqr%d" % (b % 2), pr.names["accw"])
                    return go
                for j in range(2):
                    panel(ksrc(w, k0, i * 512 + j * 256),
                          [tile_F(0, hi, lo, 2 * j, y_ready), tile_F(1, hi, lo, 2 * j + 1, y_ready)],
                          [epi(2 * j), epi(2 * j + 1)])
            pr.loop(2, body, carry=CARRY + [("act", "sqr0", "sqr1"), ("dve", "accw")])
            pr.name("y_free", now("pe"))
            if final:
                pr.name("acc", pr.last("accw"))

        pr.dma_counter("modw0")
        pr.dma_counter("modw1")
        cnt_mod = [0]

        def mod_tile(layer, u):
            s = cnt_mod[0] % 2
            cnt_mod[0] += 1
            src = I["w_mod_2"][layer].rearrange("(k p) n -> p k n", p=P)[:, :, bass.ds(u * P, P)]
            pr.wait("sp", "modr%d" % s)
            pr.pin("sp")
            ml = pr.emit("sp", lambda e: e.dma_start(modw[:, s, :, :], src), ctr="modw%d" % s)
            pr.wait("pe", ml)
            pr.pin("pe")
            for k in range(KD - 1):
                pr.raw("pe", lambda e: e.matmul(psx[:, 1, bass.ds(u * 2, 2)], modw[:, s, k, :], sc2[:, k, :],
                                                start=(k == 0), stop=False))
            T(lambda e: e.matmul(psx[:, 1, bass.ds(u * 2, 2)], modw[:, s, KD - 1, :], sc2[:, KD - 1, :],
                                 start=False, stop=True), name="modr%d" % s)

        pr.dma_counter("lda")

        def mixer_a(layer, j, mod_free=()):
            win, wout = I["a_w_in"][j], I["a_w_out"][j]
            wsr = vst[:].rearrange("p a n -> p (a n)").rearrange("p (g n) -> p g n", g=8)
            new_phase()
            pr.wait("sp", *mod_free)
            m_ws = pr.emit("act", lambda e: e.dma_start(wsr, I["a_w_s"][j].rearrange("g i j -> i g j")), ctr="lda")
            m_ws = pr.emit("act", lambda e: e.dma_start(bA[:].rearrange("p g n -> p (g n)"),
                                                        I["a_b_s"][j].rearrange("g i -> (g i)").partition_broadcast(P)), ctr="lda")
            norm(lambda k: pc("norm_gain", layer * KD + k), free="h_free")
            pr.name("acc_read", pr.last("rsr0"))
            m = G(lambda e: e.affine_select(out=wsr, in_=wsr, compare_op=ALU.is_ge, fill=0.0, base=0,
                                            pattern=[[0, 8], [-1, P]], channel_multiplier=1), m_ws)
            pr.wait("pe", m)
            for g in range(8):
                b = 2 + g // 4
                pr.wait("pe", "relx%d" % b)
                m = T(lambda e: e.transpose(psx[:, b, (g % 4) * P:(g % 4) * P + P], wsr[:, g, :], ident[:]))
                if g % 4 == 3:
                    m = V(lambda e: e.tensor_copy(wsT[:, g - 3:g + 1, :].rearrange("p g n -> p (g n)"), psx[:, b, :]), m,
                          name="relx%d" % b)
            pr.name("vst0", m)
            pr.name("vst1", m)
            V(lambda e: e.memset(ssA[:, 0:4], 0.0), name="ssA")
            pr.wait("pe", "sc2", "relx1")
            pr.wait("dve", m_ws)

            def v_body(i):
                def epi(q, pair, b):
                    def go(m):
                        for jj, t in enumerate(pair):
                            A(lambda e: e.activation(sq[:, jj, 0:256], ps[b][:, jj * 256:(jj + 1) * 256], ACT.Square,
                                                     accum_out=ssA[:, 4 + 4 * q + t:5 + 4 * q + t]),
                              m, "ssr%d" % q, "sqa%d" % jj, name="sqa%d" % jj)
                        for jj, t in enumerate(pair):
                            mv = V(lambda e: e.tensor_scalar(vA[:, t, bass.ds(i * 512 + q * 256, 256)],
                                                             ps[b][:, jj * 256:(jj + 1) * 256], 1.0, None, ALU.mult), "sqa1")
                        pr.name("rel%d" % b, mv)
                        if b % 2:
                            V(lambda e: e.tensor_tensor(ssA[:, 0:4], ssA[:, 0:4], ssA[:, 4 + 4 * q:8 + 4 * q], ALU.add),
                              "sqa1", "ssA", name="ssA")
                            pr.name("ssr%d" % q, pr.names["ssA"])
                    return go
                for q in range(2):
                    panel(ksrc(win, 0, AW + i * 512 + q * 256),
                          [tile_T((0, 1), Ah, Al, 2 * q, h_ready), tile_T((2, 3), Ah, Al, 2 * q + 1, h_ready)],
                          [epi(q, (0, 1), 2 * q), epi(q, (2, 3), 2 * q + 1)])
                    mod_tile(j, i * 4 + 2 * q)
                    mod_tile(j, i * 4 + 2 * q + 1)
            carry_mod = [("sp", "modr0", "modr1")]
            pr.loop(4, v_body, carry=CARRY + carry_mod + [("act", "ssr0", "ssr1", "sqa0", "sqa1"), ("dve", "ssA")])
            m = A(lambda e: e.activation(ssA[:, 12:16], ssA[:, 0:4], ACT.Sqrt, bias=eps[:, 0:1], scale=1.0 / AW), "ssA")
            m_rv = V(lambda e: e.reciprocal(ssA[:, 12:16], ssA[:, 12:16]), m)
            rv = ssA[:, 12:16]

            for half in range(2):
                def body(i):
                    def epi_z(f):
                        def go(m):
                            A(lambda e: e.activation(szA[:, f, :], ps[f][:], ACT.Silu), m, "szr%d" % f, name="rel%d" % f)
                        return go

                    def epi_u(f):
                        def go(m):
                            pr.name("ut%d" % f, m)
                        return go
                    q = i + half * 4
                    for f in range(2):
                        vt = V(lambda e: e.tensor_tensor(vst[:, f, :].rearrange("p (t n) -> p t n", t=TT),
                                                         vA[:, :, bass.ds(q * 256 + f * P, P)],
                                                         rv.rearrange("p (t a) -> p t a", a=1).to_broadcast([P, TT, P]), ALU.mult),
                               m_rv, "vst%d" % f, name="vsw%d" % f)
                    panel(ksrc(win, 0, 2 * AW + q * 256), [tile_F(0, Ah, Al, 0), tile_F(1, Ah, Al, 1)], [epi_z(0), epi_z(1)])
                    mod_tile(j, 16 + half * 16 + i * 4)
                    mod_tile(j, 16 + half * 16 + i * 4 + 1)
                    for f in range(2):
                        pr.wait("pe", "vsw%d" % f, "relx%d" % (2 * f))
                        pr.pin("pe")
                        for t in range(TT):
                            fn = lambda e: e.matmul(psx[:, 2 * f, t * P:(t + 1) * P], vst[:, f, t * P:(t + 1) * P],
                                                    wsT[:, bass.ds(q, 1), :].rearrange("p a n -> p (a n)"), start=True, stop=True)
                            if t < TT - 1:
                                pr.raw("pe", fn)
                            else:
                                T(fn, name="vst%d" % f)
                    m_mix = [pr.names["vst0"], pr.names["vst1"]]
                    panel(ksrc(win, 0, q * 256), [tile_F(0, Ah, Al, 2), tile_F(1, Ah, Al, 3)], [epi_u(0), epi_u(1)])
                    mod_tile(j, 16 + half * 16 + i * 4 + 2)
                    mod_tile(j, 16 + half * 16 + i * 4 + 3)
                    pend = []
                    for f in range(2):
                        gcol = PK[:, bass.ds(col["a_v_gain"] + j * 16 + q * 2 + f, 1)]
                        bb = bA[:, bass.ds(q, 1), :].to_broadcast([P, TT, P])
                        y = tmp[:, f, :]
                        y3 = y.rearrange("p (t n) -> p t n", t=TT)
                        m = V(lambda e: e.scalar_tensor_tensor(y3, psx[:, 2 * f, :].rearrange("p (t n) -> p t n", t=TT), gcol, bb,
                                                               ALU.mult, ALU.add), m_mix[f], "tmp%d" % f, name="relx%d" % (2 * f))
                        m = V(lambda e: e.tensor_tensor(y, y, szA[:, f, :], ALU.mult), m, "rel%d" % f, name="szr%d" % f)
                        m = V(lambda e: e.tensor_tensor(y, y, ps[2 + f][:], ALU.mult), m, "ut%d" % f, name="rel%d" % (2 + f))
                        mh = Ad(lambda e: e.activation(Yh[:, bass.ds(i * 2 + f, 1), :], y.rearrange("p (a n) -> p a n", a=1), ACT.Copy), m)
                        pend.append((f, mh))
                    for f, mh in pend:
                        y = tmp[:, f, :].rearrange("p (a n) -> p a n", a=1)
                        V(lambda e: e.tensor_tensor(Yl[:, bass.ds(i * 2 + f, 1), :], y, Yh[:, bass.ds(i * 2 + f, 1), :].bitcast(F32),
                                                    ALU.subtract), mh, name="tmp%d" % f)
                pr.wait("act", "y_free")
                pr.wait("dve", "y_free")
                pr.loop(4, body, carry=CARRY + carry_mod + [("act", "szr0", "szr1"), ("dve", "vst0", "vst1", "tmp0", "tmp1"),
                                                            ("pe", "relx0", "relx2")])
                for k in range(KD):
                    pr.name("y%d" % k, now("dve"))
                pr.name("h_free", now("pe"))
                out_product(wout, half * KD, half == 1)
            m = V(lambda e: e.tensor_tensor(mod[:, 48 * j:48 * j + 48, :], psx[:, 1, 0:96].rearrange("p (u a) -> p u a", a=2),
                                            PK[:, col["b_mod_2"] + 48 * j:col["b_mod_2"] + 48 * j + 48].rearrange("p (u a) -> p u a", a=1)
                                            .to_broadcast([P, 48, 2]), ALU.add), "modr0", "modr1", name="relx1")

        def split_tile(src, m, k, hi=None, lo=None, dyn=False, slot=None, name=None):
            hi = Yh if hi is None else hi
            lo = Yl if lo is None else lo
            s3 = src.rearrange("p (a n) -> p a n", a=1)
            mh = (Ad if dyn else A)(lambda e: e.activation(hi[:, bass.ds(k, 1), :], s3, ACT.Copy), m)
            m = V(lambda e: e.tensor_tensor(lo[:, bass.ds(k, 1), :], s3, hi[:, bass.ds(k, 1), :].bitcast(F32), ALU.subtract), mh)
            if slot:
                pr.name(slot, m)
            if name:
                pr.name(name, m)
            return m

        swap = [(i + 16) % 32 for i in range(32)]

        def rope(q, cs, m):
            n = q.shape[0]
            t = tmp[0:n, 3, :]
            m1 = Vp(lambda e: e.stream_shuffle(t, q, swap), m, "tmp3")
            m2 = V(lambda e: e.tensor_tensor(t, t, cs[:, 1, :], ALU.mult), m1)
            m3 = V(lambda e: e.tensor_tensor(q, q, cs[:, 0, :], ALU.mult), m1)
            return V(lambda e: e.tensor_tensor(q, q, t, ALU.add), m2, m3, name="tmp3")

        pr.dma_counter("ldb")
        psf = psx[:].rearrange("p b n -> p (b n)")
        tmpf = tmp[:].rearrange("p b n -> p (b n)")
        NB = [min(2, j + 1) + 2 * (j + 1) for j in range(TT)]
        MOFF = [sum(NB[:j]) * P for j in range(TT)]

        def blocks(j):
            return [(0, t) for t in range(max(0, j - 1), j + 1)] + [(g, t) for g in (1, 2) for t in range(j + 1)]

        def mixer_b():
            win, wout = I["b_w_in"][0], I["b_w_out"][0]
            new_phase()
            HM = 27 * P // 2
            qf = QB[:].rearrange("p a b n -> p (a b n)")
            pr.emit("act", lambda e: e.dma_start(PB[:, 0:HM], I["k_maskB"][:, 0:HM]), ctr="ldb")
            pr.emit("act", lambda e: e.dma_start(qf[:, 0:HM], I["k_maskB"][:, HM:2 * HM]), ctr="ldb")
            m = pr.emit("act", lambda e: e.dma_start(ropeB[:], I["k_ropeB"]), ctr="ldb")
            V(lambda e: e.tensor_copy(maskB[:, 0:HM], PB[:, 0:HM]), m)
            m = V(lambda e: e.tensor_copy(maskB[:, HM:2 * HM], qf[:, 0:HM]))
            pr.name("mask", m)
            pr.wait("dve", m)
            norm(lambda k: pc("norm_gain", KD + k), free="h_free")
            pr.name("acc_read", pr.last("rsr0"))
            scale = 1.0 / float(np.sqrt(P))

            def body(i):
                cnt = [0]
                pend = []

                def flush():
                    while pend:
                        pend.pop(0)()

                def epi_qk(dst, gain, b):
                    def go(m):
                        flush()
                        t = cnt[0]
                        cnt[0] += 1
                        r, c3, bank = t % 2, t % 3, 2 + t % 2
                        ms = A(lambda e: e.activation(sq[:, r, :], ps[b][:], ACT.Square), m, "sqr%d" % r)
                        mc = A(lambda e: e.activation(tmp[:, c3, :], ps[b][:], ACT.Copy), "tmp%d" % c3, name="rel%d" % b)

                        def rest():
                            mr = rstd(ms, None, P, r=r, bank=bank, src=sq[:, r, :])
                            pr.name("sqr%d" % r, now("pe"))
                            mq = V(lambda e: e.scalar_tensor_tensor(dst, tmp[:, c3, :], gain, rs[:, r, :], ALU.mult, ALU.mult),
                                   mr, mc, "qk_free", name="tmp%d" % c3)
                            pr.name("rsr%d" % r, mq)
                            rope(dst[0:32, :], ropeB, mq)
                        pend.append(rest)
                    return go

                def epi_v(g, pair, b):
                    def go(m):
                        flush()
                        V(lambda e: e.tensor_copy(VB[:, g, pair[0]:pair[0] + 2, :], ps[b][:].rearrange("p (t n) -> p t n", t=2)),
                          m, "qk_free", name="rel%d" % b)
                    return go

                def epi_z(f, b):
                    def go(m):
                        A(lambda e: e.activation(sq[:, f, :], ps[b][:], ACT.Silu), m, "sqr%d" % f, name="rel%d" % b)
                        pr.name("z%d" % f, pr.names["rel%d" % b])
                    return go
                nb = 0
                for g in range(3):
                    for qk, dst in ((0, QB), (1, KB)):
                        b = nb % 4
                        nb += 2
                        gn = pc("b_q_gain" if qk == 0 else "b_k_gain", g)
                        ready = h_ready if g == 0 and qk == 0 else None
                        panel(ksrc(win, 0, (qk * 3 + g) * D + i * 256), [tile_F(0, Ah, Al, b, ready), tile_F(1, Ah, Al, b + 1)],
                              [epi_qk(dst[:, g, 0, :], gn, b), epi_qk(dst[:, g, 1, :], gn, b + 1)])
                for g in range(3):
                    b = nb % 4
                    nb += 2
                    panel(ksrc(win, 0, (6 + g) * D + i * 256), [tile_T((0, 1), Ah, Al, b), tile_T((2, 3), Ah, Al, b + 1)],
                          [epi_v(g, (0, 1), b), epi_v(g, (2, 3), b + 1)])
                b = nb % 4
                panel(ksrc(win, 0, 9 * D + i * 256), [tile_F(0, Ah, Al, b), tile_F(1, Ah, Al, b + 1)],
                      [epi_z(0, b), epi_z(1, b + 1)])
                qk_done = now("dve")

                def scores(hh, j):
                    W, u = NB[j] * P, j % 2
                    po = 0 if u == 0 else 1024
                    pr.wait("pe", qk_done, "relx0", "relx1", "relx2")
                    runs = []
                    for pos, (g, t) in enumerate(blocks(j)):
                        if runs and runs[-1][1] == g and pos % 4:
                            runs[-1][3] += 1
                        else:
                            runs.append([pos, g, t, 1])
                    for n, (pos, g, t, c) in enumerate(runs):
                        fn = lambda e: e.matmul(psf[:, pos * P:(pos + c) * P], QB[:, g, hh, j * P:(j + 1) * P],
                                                KB[:, g, hh, t * P:(t + c) * P], start=True, stop=True)
                        if n < len(runs) - 1:
                            pr.raw("pe", fn)
                        else:
                            m = T(fn)
                    m = Vp(lambda e: e.tensor_tensor_reduce(PB[:, po:po + W], psf[:, 0:W], maskB[:, MOFF[j]:MOFF[j] + W], 1.0, 10 * NEG,
                                                           ALU.add, ALU.max, stB[:, u, 0:1]), m, "pb%d" % u, "st%d" % u, name="relx0")
                    pr.name("relx1", m)
                    pr.name("relx2", m)
                    m = V(lambda e: e.tensor_scalar(stB[:, u, 1:2], stB[:, u, 0:1], -scale, None, ALU.mult), m)
                    m = A(lambda e: e.activation(PB[:, po:po + W], PB[:, po:po + W], ACT.Exp, bias=stB[:, u, 1:2], scale=scale,
                                                 accum_out=stB[:, u, 2:3]), m)
                    mr = V(lambda e: e.reciprocal(stB[:, u, 3:4], stB[:, u, 2:3]), m)
                    return m, mr

                def values(hh, j, mp, mr):
                    u = j % 2
                    po = 0 if u == 0 else 1024
                    bl = blocks(j)
                    evs = []
                    for q0 in range(0, len(bl), 4):
                        q = q0 // 4
                        w = min(4, len(bl) - q0)
                        tb, nm = (psx[:, 3, :], "relx3") if q % 2 == 0 else (ps[2][:], "rel2")
                        pr.wait("pe", mp, nm)
                        for r in range(w):
                            m = T(lambda e: e.transpose(tb[:, r * P:(r + 1) * P], PB[:, po + (q0 + r) * P:po + (q0 + r + 1) * P], ident[:]))
                        if q % 2 == 0:
                            ev = V(lambda e: e.tensor_copy(tmp[:, q, 0:w * P], tb[:, 0:w * P]), m, "tmp%d" % q, name=nm)
                        else:
                            ev = A(lambda e: e.activation(tmp[:, q, 0:w * P], tb[:, 0:w * P], ACT.Copy), m, "tmp%d" % q, name=nm)
                        evs.append(ev)
                    pr.name("pb%d" % u, m)
                    pr.wait("pe", "rel0")
                    for pos, (g, t) in enumerate(bl):
                        if pos % 4 == 0:
                            pr.wait("pe", evs[pos // 4])
                        fn = lambda e: e.matmul(ps[0][:, j * P:(j + 1) * P], tmp[:, pos // 4, (pos % 4) * P:(pos % 4 + 1) * P],
                                                VB[:, g, t, hh * P:(hh + 1) * P], start=(pos == 0), stop=(pos == len(bl) - 1))
                        if pos < len(bl) - 1:
                            pr.raw("pe", fn)
                        else:
                            m = T(fn)
                    for q in range(len(evs)):
                        pr.name("tmp%d" % q, m)
                    m = V(lambda e: e.tensor_scalar(onB[:], ps[0][:, j * P:(j + 1) * P], stB[:, u, 3:4], None, ALU.mult),
                          m, mr, "on", name="rel0")
                    pr.name("st%d" % u, m)
                    pr.wait("pe", "rel1")
                    m = T(lambda e: e.transpose(ps[1][:, j * P:(j + 1) * P], onB[:], ident[:]), m, name="on")
                    if j == TT - 1:
                        m = V(lambda e: e.tensor_tensor(tmp[:, 3, :], ps[1][:], sq[:, hh, :], ALU.mult), m, "z%d" % hh, "tmp3", name="rel1")
                        pr.name("sqr%d" % hh, m)
                        split_tile(tmp[:, 3, :], m, i * 2 + hh, dyn=True, slot="tmp3")

                units = [(hh, j) for hh in range(2) for j in range(TT)]
                done = scores(*units[0])
                for n, (hh, j) in enumerate(units):
                    nxt = scores(*units[n + 1]) if n + 1 < len(units) else None
                    values(hh, j, *done)
                    done = nxt
                pr.name("qk_free", now("pe"))
            pr.loop(4, body, carry=CARRY + [("act", "sqr0", "sqr1", "tmp0", "tmp1", "tmp2", "rsr0", "rsr1"), ("pe", "relx0", "relx1", "relx2", "relx3"),
                                            ("dve", "tmp0", "tmp1", "tmp2", "tmp3", "y_free"), ("act", "y_free")])
            for k in range(KD):
                pr.name("y%d" % k, now("dve"))
            pr.name("h_free", now("pe"))
            out_product(wout, 0, True)

        pr.dma_counter("ldcc")

        def mixer_c():
            win, wout = I["c_w_in"][0], I["c_w_out"][0]
            before = [now(e) for e in ("act", "dve", "pe", "pool")]
            new_phase()
            mc = pr.emit("act", lambda e: e.dma_start(cntC[:].rearrange("p g n -> p (g n)"),
                                                      I["k_cnt"].rearrange("g n -> (g n)").partition_broadcast(P)), ctr="ldcc")
            for t in (xcC[:, 0, 0:16], xcC[:, 1, 0:16], s0C[:, 0:16], s1C[:, 0:16]):
                mz = V(lambda e: e.memset(t, 0.0))
            norm(lambda k: pc("norm_gain", 2 * KD + k), free="h_free")
            pr.name("acc_read", pr.last("rsr0"))
            pr.wait("dve", mc, mz)
            for g in range(4):
                def epi_x(n, b):
                    def go(m):
                        r = n % 2
                        m = A(lambda e: e.activation(xcC[:, r, 16:], ps[b][:], ACT.Copy), m, "xcr%d" % r, name="rel%d" % b)
                        src = xcC[:, r, :]
                        for step in range(g + 1):
                            dst = (s0C, s1C)[step % 2]
                            sh = 1 << step
                            m = V(lambda e: e.tensor_tensor(dst[:, 16:], src[:, 16:], src[:, 16 - sh:16 + S - sh], ALU.add), m)
                            src = dst
                        m = V(lambda e: e.tensor_tensor(tmp[:, n, :], src[:, 16:], cntC[:, g, :], ALU.mult), m, "tmp%d" % n)
                        m = V(lambda e: e.tensor_tensor(tmp[:, n, :], tmp[:, n, :], xcC[:, r, 16:], ALU.subtract), m, name="xcr%d" % r)
                        pr.wait("act", "c_free")
                        pr.wait("dve", "c_free")
                        split_tile(tmp[:, n, :], m, n, Ch, Cl, slot="tmp%d" % n, name="c%d" % n)
                    return go

                def epi_z(n, b):
                    def go(m):
                        A(lambda e: e.activation(szC[:, n, :], ps[b][:], ACT.Silu), m, "szr%d" % n, name="rel%d" % b)
                        pr.name("z%d" % n, pr.names["rel%d" % b])
                    return go

                def epi_y(n, b):
                    def go(m):
                        m = V(lambda e: e.scalar_tensor_tensor(tmp[:, n, :], ps[b][:], pc("c_scale", 4 * g + n), szC[:, n, :],
                                                               ALU.mult, ALU.mult), m, "z%d" % n, "tmp%d" % n, name="rel%d" % b)
                        pr.name("szr%d" % n, m)
                        pr.wait("act", "y_free")
                        pr.wait("dve", "y_free")
                        split_tile(tmp[:, n, :], m, (g % 2) * 4 + n, slot="tmp%d" % n, name="y%d" % ((g % 2) * 4 + n))
                    return go
                for part, epi in ((0, epi_x), (AW, epi_z)):
                    for j in range(2):
                        panel(ksrc(win, 0, part + g * 512 + j * 256), [tile_F(0, Ah, Al, 2 * j, h_ready), tile_F(1, Ah, Al, 2 * j + 1, h_ready)],
                              [epi(2 * j, 2 * j), epi(2 * j + 1, 2 * j + 1)])
                pr.name("h_free", now("pe"))
                panel(I["c_w_grp"][0][g].rearrange("(k p) n -> p k n", p=P),
                      [tile_F(n, Ch, Cl, n, lambda k: "c%d" % k, kt=4) for n in range(4)], [epi_y(n, n) for n in range(4)])
                pr.name("c_free", now("pe"))
                if g % 2:
                    out_product(wout, (g // 2) * KD, g == 3)
            return before

        def product_to_yt(w, k0, bias=None, add=False, squares=False, loops=True, more=True):
            if squares:
                V(lambda e: e.memset(acc[:], 0.0), "acc_read", name="accw")

            def body(i, more=True):
                def epi(b):
                    def go(m):
                        n = i * 4 + b
                        p3 = ps[b][:].rearrange("p (a n) -> p a n", a=1)
                        if add:
                            mx = V(lambda e: e.tensor_tensor(yt[:, bass.ds(n, 1), :], yt[:, bass.ds(n, 1), :], p3, ALU.add), m, "ytw", name="rel%d" % b)
                        elif bias:
                            mx = V(lambda e: e.tensor_scalar(yt[:, bass.ds(n, 1), :], p3, PK[:, bass.ds(col[bias] + n, 1)], None, ALU.add),
                                   m, name="rel%d" % b)
                        else:
                            mx = V(lambda e: e.tensor_scalar(yt[:, bass.ds(n, 1), :], p3, 1.0, None, ALU.mult), m, name="rel%d" % b)
                        if squares:
                            ms = Ad(lambda e: e.activation(sq[:, b % 2, :].rearrange("p (a n) -> p a n", a=1), yt[:, bass.ds(n, 1), :],
                                                           ACT.Square), mx, "sqr%d" % (b % 2))
                            V(lambda e: e.tensor_tensor(acc[:], acc[:], sq[:, b % 2, :], ALU.add), ms, "accw", name="accw")
                            pr.name("sqr%d" % (b % 2), pr.names["accw"])
                    return go
                for j in range(2):
                    panel(ksrc(w, k0, i * 512 + j * 256), [tile_F(0, Yh, Yl, 2 * j, y_ready), tile_F(1, Yh, Yl, 2 * j + 1, y_ready)],
                          [epi(2 * j), epi(2 * j + 1)], more or j == 0)
            car = CARRY + ([("act", "sqr0", "sqr1"), ("dve", "accw")] if squares else [])
            if more:
                pr.loop(2, body, carry=car)
            else:
                body(0)
                body(1, False)
            if squares:
                pr.name("acc", pr.last("accw"))
            pr.name("y_free", now("pe"))

        def post(l, which, last=False):
            m = rstd("acc", None, D, src=acc[:])
            m_acc = V(lambda e: e.memset(acc[:], 0.0), "relx3")
            for k in range(KD):
                t = tmp[:, k % 4, :]
                mt = V(lambda e: e.scalar_tensor_tensor(t, yt[:, k, :], GC[:, l, which, k:k + 1], rs[:, 0, :], ALU.mult, ALU.mult),
                       m, "tmp%d" % (k % 4))
                mx = V(lambda e: e.tensor_tensor(x[:, k, :], x[:, k, :], t, ALU.add), mt, name="tmp%d" % (k % 4))
                pr.name("xw%d" % k, mx)
                if last:
                    continue
                ms = A(lambda e: e.activation(sq[:, k % 2, :], x[:, k, :], ACT.Square), mx, "sqr%d" % (k % 2))
                if k:
                    m_acc = V(lambda e: e.tensor_tensor(acc[:], acc[:], sq[:, (k - 1) % 2, :], ALU.add), ms_old, m_acc, name="sqr%d" % ((k - 1) % 2))
                ms_old = ms
            pr.name("rsr0", mt)
            if not last:
                m_acc = V(lambda e: e.tensor_tensor(acc[:], acc[:], sq[:, 1, :], ALU.add), ms_old, m_acc, name="sqr1")
                pr.name("acc", m_acc)

        def merged_gains():
            def mcol(l, c, who=0):
                return mod[:, 48 * l + 8 * c:48 * l + 8 * c + 8, who]
            for l in range(2):
                for w, name, c in ((0, "norm_mix_pre_2", 1), (1, "norm_mix_post_2", 2), (2, "norm_mlp_pre_2", 4), (3, "norm_mlp_post_2", 5)):
                    g = PK[:, col[name] + KD * l:col[name] + KD * l + KD]
                    V(lambda e: e.scalar_tensor_tensor(GC[:, l, w, :], mcol(l, c), 1.0 if w % 2 == 0 else 0.0, g, ALU.add, ALU.mult))
            g = PK[:, col["norm_mix_pre_2"]:col["norm_mix_pre_2"] + KD]
            V(lambda e: e.scalar_tensor_tensor(GC[:, 0, 4, :], mcol(0, 1, 1), 1.0, g, ALU.add, ALU.mult))
            m = V(lambda e: e.tensor_scalar(GC[:, 1, 4, 0:1], pc("attn_subln_2", 0), 1.0 - LAM_INIT, None, ALU.mult))
            pr.wait("dve", m)
            pr.wait("act", m)

        def shift(l, c, who=0):
            return lambda k: mod[:, 48 * l + 8 * c + k, who:who + 1]

        pr.dma_counter("ldd")

        def attention2():
            win, wout = I["attn_w_qkv_2"][0], I["attn_w_out_2"][0]
            new_phase()
            merged_gains()
            lamD = PD[:, 0, 0:256].rearrange("p (a n) -> p a n", a=4)
            for t in range(CT):
                pr.emit("act", lambda e: e.dma_start(QD[:, 2 * t:2 * t + 2, :].rearrange("p a n -> p (a n)"),
                                                     I["ctx_2"][0, t * P:(t + 1) * P, :]), ctr="ldd")
            pr.emit("act", lambda e: e.dma_start(ropeD[:], I["k_ropeD"]), ctr="ldd")
            ml = pr.emit("act", lambda e: e.dma_start(PD[:, 0, 0:256],
                                                      I["attn_lambda_2"][0].rearrange("a n -> (a n)").partition_broadcast(P)), ctr="ldd")
            norm(lambda k: GC[:, 0, 0, k:k + 1], shift(0, 0), free="h_free")
            pr.wait("dve", ml)
            m = V(lambda e: e.tensor_tensor_reduce(lamD[:, 0, :], lamD[:, 0, :], lamD[:, 1, :], 1.0, 0.0, ALU.mult, ALU.add, stD[:, 16:17]))
            m = V(lambda e: e.tensor_tensor_reduce(lamD[:, 2, :], lamD[:, 2, :], lamD[:, 3, :], 1.0, 0.0, ALU.mult, ALU.add, stD[:, 17:18]))
            m = A(lambda e: e.activation(stD[:, 18:20], stD[:, 16:18], ACT.Exp), m)
            nlam = stD[:, 20:21]
            m = V(lambda e: e.scalar_tensor_tensor(nlam, stD[:, 19:20], -LAM_INIT, stD[:, 18:19], ALU.add, ALU.subtract), m)
            xctx = KDt[:].rearrange("p a n -> p (a n)")[:, 0:KD * CTX].rearrange("p (k n) -> p k n", k=KD)
            cst = QD[:].rearrange("p (t a) n -> p t (a n)", t=CT)
            pr.wait("pe", ml)
            m_acc = V(lambda e: e.memset(acc[:], 0.0), "rsr0")
            for k in range(KD):
                b = k % 2
                pr.wait("pe", "rel%d" % b)
                for t in range(CT):
                    m = T(lambda e: e.transpose(ps[b][:, t * P:(t + 1) * P], cst[:, t, k * P:(k + 1) * P], ident[:]))
                m = V(lambda e: e.tensor_copy(xctx[:, k, :], ps[b][:, 0:CTX]), m, name="rel%d" % b)
                ms = A(lambda e: e.activation(sq[:, b, 0:CTX], xctx[:, k, :], ACT.Square), m, "sqr%d" % b)
                m_acc = V(lambda e: e.tensor_tensor(acc[:, 0:CTX], acc[:, 0:CTX], sq[:, b, 0:CTX], ALU.add), ms, m_acc, name="sqr%d" % b)
            pr.name("acc", m_acc)
            norm(lambda k: GC[:, 0, 4, k:k + 1], shift(0, 0, 1), xctx, Uh, Ul, free="relx3", cols=CTX, tag="u")
            pr.name("qk_free", now("dve"))
            pr.name("acc_read", pr.last("rsr0"))

            def body(i):
                def epi_lat(dst, b):
                    def go(m):
                        m = A(lambda e: e.activation(dst, ps[b][:], ACT.Copy), m, "qk_free", name="rel%d" % b)
                        rope(dst, ropeD, m)
                    return go

                def epi_ctx(dst, b):
                    def go(m):
                        V(lambda e: e.tensor_copy(dst, ps[b][:, 0:CTX]), m, "qk_free", name="rel%d" % b)
                    return go

                def epi_v(t0, c0, b):
                    def go(m):
                        V(lambda e: e.tensor_copy(VD[:, t0:t0 + 2, c0:c0 + 256], ps[b][:].rearrange("p (t n) -> p t n", t=2)),
                          m, "qk_free", name="rel%d" % b)
                    return go

                def u_ready(k):
                    return "u%d" % k
                for j in range(2):
                    panel(ksrc(win, 0, i * 512 + j * 256), [tile_F(0, Ah, Al, 2 * j, h_ready), tile_F(1, Ah, Al, 2 * j + 1, h_ready)],
                          [epi_lat(QD[:, 2 * j, :], 2 * j), epi_lat(QD[:, 2 * j + 1, :], 2 * j + 1)])
                for j in range(2):
                    h0, h1 = 2 * j, 2 * j + 1
                    panel(ksrc(win, 0, D + i * 512 + j * 256),
                          [tile_F(0, Ah, Al, 0), tile_F(0, Uh, Ul, 1, u_ready, cols=CTX), tile_F(1, Ah, Al, 2), tile_F(1, Uh, Ul, 3, cols=CTX)],
                          [epi_lat(KDt[:, h0, CTX:], 0), epi_ctx(KDt[:, h0, 0:CTX], 1), epi_lat(KDt[:, h1, CTX:], 2),
                           epi_ctx(KDt[:, h1, 0:CTX], 3)])
                for j in range(2):
                    panel(ksrc(win, 0, 2 * D + i * 512 + j * 256),
                          [tile_T((0, 1), Uh, Ul, 0), tile_T((0, 1), Ah, Al, 1), tile_T((2, 3), Ah, Al, 2)],
                          [epi_v(0, j * 256, 0), epi_v(2, j * 256, 1), epi_v(4, j * 256, 2)])
                qk_done = now("dve")
                NK = S + CTX

                def scores(h, j):
                    o = 8 * (j % 2)
                    out_m = []
                    for p in range(2):
                        pr.wait("pe", qk_done, "relx%d" % (2 * p), "relx%d" % (2 * p + 1))
                        q = QD[64 * p:64 * p + 64, h, j * P:(j + 1) * P]
                        c = 2 * p * S
                        pr.raw("pe", lambda e: e.matmul(psf[:, c:c + S], q, KDt[64 * p:64 * p + 64, h, 0:S], start=True, stop=True))
                        m = T(lambda e: e.matmul(psf[:, c + S:c + NK], q, KDt[64 * p:64 * p + 64, h, S:NK], start=True, stop=True))
                        m = V(lambda e: e.tensor_reduce(stD[:, o + p:o + p + 1], psf[:, c:c + NK], AX.X, ALU.max), m, "st%d" % (j % 2))
                        m = V(lambda e: e.tensor_scalar(stD[:, o + 2 + p:o + 3 + p], stD[:, o + p:o + p + 1], -0.125, None, ALU.mult), m)
                        m = A(lambda e: e.activation(PD[:, p, :], psf[:, c:c + NK], ACT.Exp, bias=stD[:, o + 2 + p:o + 3 + p], scale=0.125,
                                                     accum_out=stD[:, o + 4 + p:o + 5 + p]), m, "pd", name="relx%d" % (2 * p))
                        pr.name("relx%d" % (2 * p + 1), m)
                    m = V(lambda e: e.reciprocal(stD[:, o + 6:o + 8], stD[:, o + 4:o + 6]), m)
                    return V(lambda e: e.tensor_tensor(stD[:, o + 7:o + 8], stD[:, o + 7:o + 8], nlam, ALU.mult), m)

                def combine(h, j, m):
                    o = 8 * (j % 2)
                    m = V(lambda e: e.tensor_scalar(PD[:, 1, :], PD[:, 1, :], stD[:, o + 7:o + 8], None, ALU.mult), m)
                    m = V(lambda e: e.scalar_tensor_tensor(tmpf[:, 0:NK], PD[:, 0, :], stD[:, o + 6:o + 7], PD[:, 1, :], ALU.mult, ALU.add),
                          m, "tmp0", "tmp1", name="pd")
                    pr.name("st%d" % (j % 2), m)
                    return m

                def values(h, j, ma):
                    pr.wait("pe", ma, "rel0")
                    for t in range(4):
                        m = T(lambda e: e.transpose(ps[0][:, t * P:(t + 1) * P], tmpf[:, t * P:(t + 1) * P], ident[:]))
                    e0 = A(lambda e: e.activation(tmp[:, 2, :], ps[0][:], ACT.Copy), m, "tmp2", name="rel0")
                    pr.wait("pe", "rel1")
                    for t in range(2):
                        m = T(lambda e: e.transpose(ps[1][:, t * P:(t + 1) * P], tmpf[:, (4 + t) * P:(5 + t) * P], ident[:]))
                    pr.name("tmp0", m)
                    pr.name("tmp1", m)
                    e1 = V(lambda e: e.tensor_copy(tmp[:, 3, 0:256], ps[1][:, 0:256]), m, "tmp3", name="rel1")
                    pr.wait("pe", "rel2")
                    for t in range(6):
                        if t in (0, 4):
                            pr.wait("pe", e0 if t == 0 else e1)
                        fn = lambda e: e.matmul(ps[2][:, j * P:(j + 1) * P], VD[:, t, h * P:(h + 1) * P],
                                                tmpf[:, 1024 + t * P:1024 + (t + 1) * P], start=(t == 0), stop=(t == 5))
                        if t < 5:
                            pr.raw("pe", fn)
                        else:
                            m = T(fn, name="tmp2")
                    pr.name("tmp3", m)
                    if j == TT - 1:
                        r = h % 2
                        A(lambda e: e.activation(sq[:, r, :], ps[2][:], ACT.Square), m, "sqr%d" % r)
                        ms = A(lambda e: e.activation(acc[:], ps[2][:], ACT.Copy), "acch", name="rel2")
                        m = T(lambda e: e.matmul(ps[3][:], ones[:], sq[:, r, :], start=True, stop=True), ms, "rel3", name="sqr%d" % r)
                        m = A(lambda e: e.activation(rs[:, 0, :], ps[3][:], ACT.Sqrt, bias=eps[:, 0:1], scale=1.0 / P), m, "rsr0", name="rel3")
                        m = V(lambda e: e.reciprocal(rs[:, 0, :], rs[:, 0, :]), m)
                        m = V(lambda e: e.scalar_tensor_tensor(acc[:], acc[:], GC[:, 1, 4, 0:1], rs[:, 0, :], ALU.mult, ALU.mult), m, name="rsr0")
                        split_tile(acc[:], m, i * 4 + h, dyn=True, slot="acch")

                units = [(h, j) for h in range(4) for j in range(TT)]
                done = scores(*units[0])
                for n, (h, j) in enumerate(units):
                    ma = combine(h, j, done)
                    if n + 1 < len(units):
                        done = scores(*units[n + 1])
                    values(h, j, ma)
                pr.name("qk_free", now("pe"))
            pr.loop(2, body, carry=CARRY + [("act", "qk_free", "y_free", "tmp2", "sqr0", "sqr1", "acch", "rsr0", "pd"),
                                            ("dve", "qk_free", "y_free", "tmp0", "tmp1", "tmp3"),
                                            ("pe", "relx0", "relx1", "relx2", "relx3")])
            for k in range(KD):
                pr.name("y%d" % k, now("dve"))
            pr.name("h_free", now("pe"))
            new_phase()
            product_to_yt(wout, 0, squares=True)
            post(0, 1)

        def mlp(l, last=False):
            norm(lambda k: GC[:, l, 2, k:k + 1], shift(l, 3), free="h_free")
            pr.name("acc_read", pr.last("rsr0"))
            win, wout = I["w_mlp_in_2"][l], I["w_mlp_out_2"][l]
            V(lambda e: e.memset(yt[:], 0.0), name="ytw")

            def quarter(iq, more=True):
                def inner(i):
                    def epi(b):
                        def go(m):
                            m = A(lambda e: e.activation(tmp[:, b, :], ps[b][:], ACT.Relu), m, "tmp%d" % b, name="rel%d" % b)
                            m = V(lambda e: e.tensor_tensor(tmp[:, b, :], tmp[:, b, :], tmp[:, b, :], ALU.mult), m)
                            pr.wait("act", "y_free")
                            pr.wait("dve", "y_free")
                            split_tile(tmp[:, b, :], m, i * 4 + b, dyn=True, slot="tmp%d" % b, name="yb%d" % b)
                        return go
                    for j in range(2):
                        panel(ksrc(win, 0, iq * D + i * 512 + j * 256), [tile_F(0, Ah, Al, 2 * j, h_ready), tile_F(1, Ah, Al, 2 * j + 1, h_ready)],
                              [epi(2 * j), epi(2 * j + 1)])
                pr.loop(2, inner, carry=CARRY + [("act", "tmp0", "tmp1", "tmp2", "tmp3")])
                if not pr.dry:
                    for b in range(4):
                        m = pr.names["yb%d" % b]
                        pr.names["y%d" % (4 + b)] = m
                        pr.names["y%d" % b] = Mark(m.ctr, m.const, m.levels, m.back + m.levels[-1].per[m.ctr])
                product_to_yt(wout, iq * KD, add=True, more=more)
            pr.loop(3, quarter, carry=CARRY + [("act", "tmp0", "tmp1", "tmp2", "tmp3", "y_free"), ("dve", "y_free")])
            quarter(3, more=not last)
            pr.name("h_free", now("pe"))
            m_acc = V(lambda e: e.memset(acc[:], 0.0), "acc_read")
            for k in range(KD):
                ms = A(lambda e: e.activation(sq[:, k % 2, :], yt[:, k, :], ACT.Square), now("dve"), "sqr%d" % (k % 2))
                m_acc = V(lambda e: e.tensor_tensor(acc[:], acc[:], sq[:, k % 2, :], ALU.add), ms, m_acc, name="sqr%d" % (k % 2))
            pr.name("acc", m_acc)
            post(l, 3, last)

        pr.dma_counter("ldf")
        pr.dma_counter("stf0")
        pr.dma_counter("stf1")
        TWO_PI = 2.0 * float(np.pi)
        C1 = 6.28125
        C2 = float(np.float32(TWO_PI - C1))
        C3 = float(np.float32(TWO_PI - C1 - C2))
        MAGIC = 1.5 * 2.0 ** 23
        PI_IN = float(np.nextafter(np.float32(np.pi), np.float32(0)))

        def filters():
            new_phase()
            ld = [(zF[:], I["k_z"]), (w1F[:], I["hy_filt_w1_2"][0]), (w2F[:], I["hy_filt_w2_2"][0].rearrange("a i j -> i a j")),
                  (woF[:], I["hy_filt_w_out_2"][0]), (colF[0:64, 0:1], I["hy_filt_b1_2"][0].rearrange("(p a) -> p a", a=1)),
                  (colF[0:64, 1:2], I["hy_filt_b2_2"][0, 0].rearrange("(p a) -> p a", a=1)),
                  (colF[0:64, 2:3], I["hy_filt_b2_2"][0, 1].rearrange("(p a) -> p a", a=1)),
                  (colF[0:64, 3:4], I["hy_filt_freq_2"][0].rearrange("(p a) -> p a", a=1)),
                  (colF[:, 4:9], I["k_tcol"]), (dlF[:], I["k_delta"].partition_broadcast(P)),
                  (tabF[:, 0, :, :], I["k_tab0"][0].rearrange("(k p) n -> p k n", p=P)),
                  (tabF[:, 1, :, :], I["k_tab0"][1].rearrange("(k p) n -> p k n", p=P))]
            for d, s_ in ld:
                ml = pr.emit("act", lambda e: e.dma_start(d, s_), ctr="ldf")
            for e in ("pe", "dve", "act"):
                pr.wait(e, ml)
            m = None
            for j in range(3):
                lhs, rhs = (w1F[:], zF[:]) if j == 0 else (w2F[:, j - 1, :], hdF[:, (j - 1) % 2, :])
                pr.wait("pe", "relx0")
                m = T(lambda e: e.matmul(psx[0:64, 0, :], lhs, rhs, start=True, stop=True), *([m] if m else []))
                a, k = tmp[0:64, 0, :], kF[:]
                m = V(lambda e: e.tensor_scalar(a, psx[0:64, 0, :], colF[0:64, j:j + 1], colF[0:64, 3:4], ALU.add, ALU.mult), m, name="relx0")
                m = V(lambda e: e.tensor_scalar(k, a, 1.0 / TWO_PI, MAGIC, ALU.mult, ALU.add), m)
                m = V(lambda e: e.tensor_scalar(k, k, MAGIC, None, ALU.subtract), m)
                for c in (C1, C2, C3):
                    m = V(lambda e: e.scalar_tensor_tensor(a, k, -c, a, ALU.mult, ALU.add), m)
                m = V(lambda e: e.tensor_scalar(a, a, -PI_IN, PI_IN, ALU.max, ALU.min), m)
                m = A(lambda e: e.activation(hdF[:, j % 2, :], a, ACT.Sin), m)
            hd = hdF[:, 0, :]
            nst = [0]
            for half in range(2):
                c0 = half * 512
                for t in range(TT):
                    pr.wait("pe", m, "relx0", "relx1")
                    pr.raw("pe", lambda e: e.matmul(psx[:, 0, :], hd[:, t * P:(t + 1) * P], woF[:, c0:c0 + 512], start=True, stop=True))
                    mp = T(lambda e: e.matmul(psx[:, 1, :], hd[:, t * P:(t + 1) * P], woF[:, D + c0:D + c0 + 512], start=True, stop=True))
                    md = A(lambda e: e.activation(tmp[:, 0, :], dlF[:, c0:c0 + 512], ACT.Exp, scale=colF[:, 4 + t:5 + t]), now("dve"), now("act"))
                    m1 = V(lambda e: e.tensor_tensor(tmp[:, 1, :], psx[:, 0, :], tmp[:, 0, :], ALU.mult), mp, md, now("dve"), "hs_free", name="relx0")
                    if t == 0:
                        m2 = V(lambda e: e.scalar_tensor_tensor(tmp[:, 2, :], psx[:, 1, :], colF[:, 8:9], tmp[:, 0, :], ALU.mult, ALU.mult), name="relx1")
                    else:
                        m2 = V(lambda e: e.tensor_tensor(tmp[:, 2, :], psx[:, 1, :], tmp[:, 0, :], ALU.mult), name="relx1")
                    V(lambda e: e.tensor_tensor(hsF[:, t, :], tmp[:, 1, :], tmp[:, 2, :], ALU.add), m2)
                    mh = V(lambda e: e.tensor_tensor(hdiffF[:, t, :], tmp[:, 1, :], tmp[:, 2, :], ALU.subtract), m2)
                for fi in range(TT):
                    for w, src in ((0, hsF), (1, hdiffF)):
                        pr.wait("pe", mh, "relx%d" % (2 + w))
                        for k in range(TT):
                            fn = lambda e: e.matmul(psx[:, 2 + w, :], tabF[:, w, k, fi * P:(fi + 1) * P], src[:, k, :], start=(k == 0), stop=(k == TT - 1))
                            if k < TT - 1:
                                pr.raw("pe", fn)
                            else:
                                m3 = T(fn)
                        mk = A(lambda e: e.activation(kcF[:, w, :], psx[:, 2 + w, :], ACT.Copy, scale=1.0 / S), m3, "kst%d" % w, name="relx%d" % (2 + w))
                        pr.wait("act", mk)
                        pr.emit("act", lambda e: e.dma_start(kspec[w, fi, :, c0:c0 + 512], kcF[:, w, :]), ctr="stf%d" % w, name="kst%d" % w)
                pr.name("hs_free", now("pe"))
            pr.name("tmp0", now("dve"))

        pr.dma_counter("ldh")

        def hyena():
            win, wout = I["hy_w_in_2"][0], I["hy_w_out_2"][0]
            new_phase()
            for r in range(2):
                V(lambda e: e.memset(uH[:, r, 0:1], 0.0))
                mz = V(lambda e: e.memset(uH[:, r, S + 1:S + 2], 0.0))
            norm(lambda k: GC[:, 1, 0, k:k + 1], shift(1, 0), free="h_free")
            pr.name("acc_read", pr.last("rsr0"))
            pr.wait("dve", mz)

            def body(i):
                for jj in range(2):
                    def epi(part, f, b):
                        def go(m):
                            n = i * 4 + jj * 2 + f
                            r = b % 2
                            pcol = lambda name, o: PK[:, bass.ds(col[name] + o + n, 1)]
                            m = Ad(lambda e: e.activation(uH[:, r, 1:S + 1], ps[b][:], ACT.Identity, bias=pcol("hy_b_in_2", part * KD)),
                                   m, "uhr%d" % r, name="rel%d" % b)
                            t = tmp[:, f if part == 1 else 2 + f, :]
                            tn = "tmp%d" % (f if part == 1 else 2 + f)
                            taps = [pcol("hy_w_short_2", tap * 3 * KD + part * KD) for tap in range(3)]
                            m = V(lambda e: e.tensor_scalar(t, uH[:, r, 1:S + 1], taps[1], pcol("hy_b_short_2", part * KD), ALU.mult, ALU.add), m, tn)
                            m = V(lambda e: e.scalar_tensor_tensor(t, uH[:, r, 0:S], taps[0], t, ALU.mult, ALU.add), m)
                            last = t if part else x0H[:, bass.ds(n, 1), :].rearrange("p a n -> p (a n)")
                            m = V(lambda e: e.scalar_tensor_tensor(last, uH[:, r, 2:S + 2], taps[2], t, ALU.mult, ALU.add), m, name="uhr%d" % r)
                            if part == 0:
                                pr.name(tn, m)
                            if part == 2:
                                m = V(lambda e: e.tensor_tensor(wH[:, bass.ds(n, 1), :].rearrange("p a n -> p (a n)"), tmp[:, f, :], t, ALU.mult),
                                      m, name="tmp%d" % f)
                                pr.name("tmp%d" % (2 + f), m)
                        return go
                    for part in range(3):
                        b = 2 * ((jj * 3 + part) % 2)
                        panel(ksrc(win, 0, part * D + i * 512 + jj * 256), [tile_F(0, Ah, Al, b, h_ready), tile_F(1, Ah, Al, b + 1, h_ready)],
                              [epi(part, 0, b), epi(part, 1, b + 1)])
            pr.loop(2, body, carry=CARRY + [("act", "uhr0", "uhr1"), ("dve", "tmp0", "tmp1", "tmp2", "tmp3")])
            pr.name("h_free", now("pe"))
            new_phase()
            pr.wait("act", "kst0", "kst1")
            for w in range(2):
                m_tab = pr.emit("act", lambda e: e.dma_start(tabH[:, w, :, :], I["k_tabs"][w].rearrange("(k p) n -> p k n", p=P)), ctr="ldh")
            for half in range(2):
                c0 = half * 512
                pr.wait("act", "ks_free")
                for w in range(2):
                    for fi in range(TT):
                        m_k = pr.emit("act", lambda e: e.dma_start(kS[:, w, fi, :], kspec[w, fi, :, c0:c0 + 512]), ctr="ldh")
                for k in range(TT):
                    b = k % 4
                    pr.wait("pe", "rel%d" % b)
                    for t in range(TT):
                        m = T(lambda e: e.transpose(ps[b][:, t * P:(t + 1) * P], wH[:, 4 * half + k, t * P:(t + 1) * P], ident[:]))
                    m = V(lambda e: e.tensor_copy(wtH[:, :, k * P:(k + 1) * P], ps[b][:].rearrange("p (t n) -> p t n", t=TT)), m, "wt_free", name="rel%d" % b)
                pr.wait("pe", m, m_k)
                pr.wait("dve", m_k)
                for fi in range(TT):
                    bc, bs = 2 * (fi % 2), 2 * (fi % 2) + 1
                    for w, b in ((0, bc), (1, bs)):
                        pr.wait("pe", "rel%d" % b)
                        for k in range(TT):
                            fn = lambda e: e.matmul(ps[b][:], tabH[:, w, k, fi * P:(fi + 1) * P], wtH[:, k, :], start=(k == 0), stop=(k == TT - 1))
                            if k < TT - 1:
                                pr.raw("pe", fn)
                            else:
                                m = T(fn)
                    yr, yi, kc, ks = yS[:, 0, fi, :], yS[:, 1, fi, :], kS[:, 0, fi, :], kS[:, 1, fi, :]
                    a, t = V(lambda e: e.tensor_tensor(yr, ps[bc][:], kc, ALU.mult), m, "ys_free"), None
                    a = V(lambda e: e.tensor_tensor(tmp[:, 0, :], ps[bs][:], ks, ALU.mult), "tmp0")
                    b1 = V(lambda e: e.tensor_tensor(yi, ps[bc][:], ks, ALU.mult), name="rel%d" % bc)
                    b2 = V(lambda e: e.tensor_tensor(tmp[:, 1, :], ps[bs][:], kc, ALU.mult), "tmp1", name="rel%d" % bs)
                    V(lambda e: e.tensor_tensor(yr, yr, tmp[:, 0, :], ALU.subtract), a, name="tmp0")
                    my = V(lambda e: e.tensor_tensor(yi, yi, tmp[:, 1, :], ALU.add), b2, name="tmp1")
                pr.name("wt_free", now("pe"))
                pr.name("ks_free", my)
                for n in range(4):
                    g = 4 * half + n
                    b = n
                    pr.wait("pe", my, "rel%d" % b)
                    for w in range(2):
                        for fi in range(TT):
                            fn = lambda e: e.matmul(ps[b][:], yS[:, w, fi, n * P:(n + 1) * P], tabH[:, w, fi, :], start=(w + fi == 0), stop=(w == 1 and fi == TT - 1))
                            if w == 0 or fi < TT - 1:
                                pr.raw("pe", fn)
                            else:
                                m = T(fn)
                    t = tmp[:, 2 + n % 2, :]
                    tn = "tmp%d" % (2 + n % 2)
                    m = V(lambda e: e.scalar_tensor_tensor(t, wH[:, g, :], pc("hy_bias_2", g), ps[b][:], ALU.mult, ALU.add), m, tn, name="rel%d" % b)
                    m = V(lambda e: e.tensor_tensor(t, t, x0H[:, g, :], ALU.mult), m)
                    split_tile(t, m, g, slot=tn, name="y%d" % g)
                pr.name("ys_free", now("pe"))
            new_phase()
            product_to_yt(wout, 0, bias="hy_b_out_2", squares=True)
            post(1, 1)

        split_panel(0)
        mixer_a(0, 0)
        mixer_b()
        before_c = mixer_c()
        mixer_a(3, 1, before_c)
        filters()
        attention2()
        mlp(0)
        hyena()
        mlp(1, last=True)
        new_phase()
        pr.dma_counter("out")
        for t in range(TT):
            for q in range(2):
                b = (2 * t + q) % 4
                pr.wait("pe", "rel%d" % b)
                for k in range(4):
                    m = T(lambda e: e.transpose(ps[b][:, k * P:(k + 1) * P], x[:, 4 * q + k, t * P:(t + 1) * P], ident[:]))
                m = V(lambda e: e.tensor_copy(stage[:, t, q * 512:(q + 1) * 512], ps[b][:]), m, name="rel%d" % b)
            pr.wait("act", m)
            mo = pr.emit("act", lambda e: e.dma_start(out[0, t * P:(t + 1) * P, :], stage[:, t, :]), ctr="out")
        pr.wait("act", mo, "kst0", "kst1")


_INS = ["x", "norm_gain", "a_w_in", "a_v_gain", "a_w_s", "a_b_s", "a_w_out", "b_w_in", "b_q_gain", "b_k_gain", "b_w_out",
        "c_w_in", "c_w_grp", "c_scale", "c_w_out", "c_2", "ctx_2", "c_ctx_2", "w_mod_2", "b_mod_2", "norm_mix_pre_2",
        "norm_mix_post_2", "norm_mlp_pre_2", "norm_mlp_post_2", "w_mlp_in_2", "w_mlp_out_2", "attn_w_qkv_2", "attn_w_out_2",
        "attn_lambda_2", "attn_subln_2", "hy_w_in_2", "hy_b_in_2", "hy_w_short_2", "hy_b_short_2", "hy_filt_w1_2",
        "hy_filt_b1_2", "hy_filt_w2_2", "hy_filt_b2_2", "hy_filt_freq_2", "hy_filt_w_out_2", "hy_bias_2", "hy_w_out_2",
        "hy_b_out_2"]


def shape_constants():
    f = np.float32
    c = {"k_ident": np.eye(P, dtype=f)}
    def rope(freq_rows, pos):
        ang = (pos[None, :].astype(f) * freq_rows[:, None].astype(f)).astype(f)
        return np.cos(ang).astype(f), np.sin(ang).astype(f)
    inv = np.power(f(500000.0), -np.arange(16, dtype=f) / f(16)).astype(f)
    pos = np.arange(S, dtype=f)
    co, si = rope(inv, pos)
    c["k_ropeB"] = np.stack([np.concatenate([co, co]), np.concatenate([-si, si])], axis=1)
    inv = (f(10000.0) ** (-np.arange(16, dtype=f) / f(16))).astype(f)
    blocks = []
    for p in (np.repeat(np.arange(S // 64), 64), np.tile(np.arange(64), S // 64)):
        co, si = rope(inv, p)
        blocks.append(np.stack([np.concatenate([co, co]), np.concatenate([-si, si])], axis=1))
    c["k_ropeD"] = np.concatenate(blocks * 2, axis=0)
    out = []
    q = np.arange(P)[:, None]
    for j in range(TT):
        for g, (span, dil) in enumerate(((128, 1), (512, 4), (2048, 16))):
            for t in range(max(0, j - 1) if g == 0 else 0, j + 1):
                d = (j * P + q) - (t * P + np.arange(P)[None, :])
                out.append(np.where((d >= 0) & (d <= span) & (d % dil == 0), 0.0, NEG))
    c["k_maskB"] = np.concatenate(out, axis=1)
    c["k_cnt"] = np.stack([1.0 / np.minimum(np.arange(S) + 1, w) for w in (2, 4, 8, 16)])
    t = np.linspace(0.0, 1.0, S, dtype=f)[:, None]
    w = (2.0 * np.pi * np.arange(S, dtype=f)[:, None] / S).astype(f)
    fr = np.linspace(1e-4, 15, 16, dtype=f)[None, :]
    c["k_z"] = np.concatenate([t, np.cos(fr * w), -np.sin(fr * w)], axis=-1).T
    tc = np.zeros((P, 5))
    tc[:, 0:4] = -t.reshape(TT, P).T
    tc[1:, 4] = 1.0
    c["k_tcol"] = tc
    c["k_delta"] = np.abs(np.linspace(np.log(1e-2) / 1.5, np.log(1e-2) / 0.3, D, dtype=f))
    fq = (np.arange(S) + 0.5)
    a = 2 * np.pi * np.outer(np.arange(S), fq) / (2 * S)
    c["k_tab0"] = np.stack([np.cos(a), np.sin(a)])
    a = 2 * np.pi * np.outer(np.arange(S) + 0.5, fq) / (2 * S)
    c["k_tabs"] = np.stack([np.cos(a), np.sin(a)])
    return {n: np.ascontiguousarray(v.astype(f)) for n, v in c.items()}


def kernel(**inputs):
    import concourse.bacc as _bacc
    from concourse.bass_utils import run_bass_kernel_spmd as _run

    nc = _bacc.Bacc("TRN2", target_bir_lowering=False, num_devices=1)
    arrays, aps = {}, {}
    given = {n: np.ascontiguousarray(inputs[n]) for n in _INS}
    given.update(shape_constants())
    for name, a in given.items():
        arrays[f"in_{name}_dram"] = a
        aps[name] = nc.dram_tensor(f"in_{name}_dram", a.shape, mybir.dt.from_np(a.dtype), kind="ExternalInput").ap()
    out = nc.dram_tensor("out_0_dram", (1, S, D), F32, kind="ExternalOutput").ap()
    build(nc, aps, out)
    r = _run(nc, [arrays], core_ids=[0])
    return r.results[0]["out_0_dram"]
```

```python
from contextlib import ExitStack

import numpy as np

import concourse.bass as bass
from concourse import mybir

F32 = mybir.dt.float32
F32R = mybir.dt.float32r
BF16 = mybir.dt.bfloat16
ALU = mybir.AluOpType
ACT = mybir.ActivationFunctionType
AX = mybir.AxisListType

P = 128
S = 512
D = 1024
KD = D // P
TT = S // P
CTX = 256
CT = CTX // P
AW = 2 * D
DFF = 4 * D
NEG = -1e30
EPS = 1e-6
LAM_INIT = 0.8 - 0.6 * float(np.exp(-0.3 * 0))
CREDIT = 4096


class Mark:

    def __init__(self, ctr, const, levels, back=0):
        self.ctr, self.const, self.levels, self.back = ctr, const, levels, back


class Counter:
    def __init__(self, sem, step, start=0):
        self.sem, self.step, self.const = sem, step, start


class Loop:
    def __init__(self, i, n, per, start, table):
        self.i, self.n, self.per, self.start, self.table = i, n, per, start, table
        self.seen = set()


class Program:

    def __init__(self, nc, sem):
        self.nc, self.sem = nc, sem
        self.eng = {"pe": nc.tensor, "act": nc.scalar, "dve": nc.vector, "pool": nc.gpsimd, "sp": nc.sync}
        self.ctr = {}
        for n in ("pe", "act", "dve", "pool"):
            self.ctr[n] = Counter(sem("done_" + n), 1, CREDIT)
        for n in ("pe", "act", "dve", "pool"):
            self.ctr["norm_" + n] = Counter(sem("norm_" + n), 1)
        self.pins = sem("pins")
        self.asked = {e: [] for e in self.eng}
        self.loops = []
        self.names = {}
        self.dry = 0
        self.drytab = None

    def credit(self):
        for n in ("pe", "act", "dve", "pool"):
            self.eng[n].sem_inc(self.ctr[n].sem, CREDIT)

    def dma_counter(self, name):
        self.ctr[name] = Counter(self.sem(name), 16)
        return name

    def emit(self, e, fn, ctr=None, name=None):
        c = self.ctr[ctr or e]
        if not self.dry:
            self.put_waits(e)
            fn(self.eng[e]).then_inc(c.sem, c.step)
        c.const += c.step
        m = Mark(c, c.const, tuple(self.loops))
        if name:
            self.name(name, m)
        return m

    def raw(self, e, fn):
        if not self.dry:
            self.put_waits(e)
            fn(self.eng[e])

    def name(self, name, m):
        self.names[name] = m
        if self.dry and self.drytab is not None:
            self.drytab[name] = (m.ctr, m.const - self.drystart[m.ctr])
        elif self.loops:
            self.loops[-1].seen.add(name)

    def last(self, name):
        if self.dry:
            return self.names.get(name)
        if self.loops:
            lp = self.loops[-1]
            if name not in lp.seen and name in lp.table:
                ctr, rel = lp.table[name]
                return Mark(ctr, lp.start[ctr] + rel, tuple(self.loops), back=lp.per[ctr])
        return self.names.get(name)

    def value(self, m):
        v = m.const - m.back
        out = None
        for lp in m.levels:
            per = lp.per[m.ctr]
            if lp in self.loops:
                if per:
                    term = lp.i * per
                    out = term if out is None else out + term
            else:
                v += per * (lp.n - 1)
        return v if out is None else out + v

    def wait(self, e, *marks):
        if self.dry:
            return
        for m in marks:
            if isinstance(m, str):
                m = self.last(m)
            if m is not None:
                self.asked[e].append((m.ctr, self.value(m), (m.levels, m.const - m.back)))

    def put_waits(self, e):
        asked, self.asked[e] = self.asked[e], []
        furthest = {}
        for c, v, (levels, at) in asked:
            if (c, levels) not in furthest or at > furthest[c, levels][0]:
                furthest[c, levels] = (at, v)
        seen = set()
        for (c, _), (_, v) in furthest.items():
            if c in seen:
                self.eng[e].sem_inc(self.pins, 1)
                seen = set()
            seen.add(c)
            self.eng[e].wait_ge(c.sem, v)

    def loop(self, n, body, carry=()):
        for e, *names in carry:
            self.wait(e, *[x for x in names if x in self.names])
            if self.loops:
                self.pin(e)
        ctrs = list(self.ctr.values())
        saved_names, saved_tab, saved_start = dict(self.names), self.drytab, (self.drystart if self.dry else None)
        start = {c: c.const for c in ctrs}
        self.dry += 1
        self.drytab, self.drystart = {}, start
        body(0)
        table = self.drytab
        per = {c: c.const - start[c] for c in ctrs}
        self.dry -= 1
        self.drytab, self.drystart = saved_tab, saved_start
        if self.dry:
            for c in ctrs:
                c.const = start[c] + per[c] * n
            for k, (c, rel) in table.items():
                self.drytab[k] = (c, start[c] + per[c] * (n - 1) + rel - self.drystart[c])
            return
        for c in ctrs:
            c.const = start[c]
        self.names = saved_names
        for e in self.eng:
            self.put_waits(e)
        with self.nc.Fori(0, n) as i:
            self.loops.append(Loop(i, n, per, start, table))
            body(i)
            for e in self.eng:
                self.put_waits(e)
            self.loops.pop()
        for c in ctrs:
            c.const = start[c] + per[c] * n
        if self.loops:
            self.loops[-1].seen.update(table)

    def A(self, fn, *waits, name=None):
        self.wait("act", *waits)
        return self.emit("act", fn, name=name)

    def pin(self, e):
        if not self.dry:
            self.put_waits(e)
            self.eng[e].sem_inc(self.pins, 1)

    def Adyn(self, fn, *waits, name=None):
        self.wait("act", *waits)
        self.pin("act")
        return self.emit("act", fn, name=name)

    def Vpin(self, fn, *waits, name=None):
        self.wait("dve", *waits)
        self.pin("dve")
        return self.emit("dve", fn, name=name)

    def V(self, fn, *waits, name=None):
        self.wait("dve", *waits)
        return self.emit("dve", fn, name=name)

    def G(self, fn, *waits, name=None):
        self.wait("pool", *waits)
        return self.emit("pool", fn, name=name)

    def T(self, fn, *waits, name=None):
        self.wait("pe", *waits)
        return self.emit("pe", fn, name=name)


PACKS = [
    [("norm_gain", 4 * KD), ("a_v_gain", 2 * AW // P), ("c_scale", AW // P), ("b_q_gain", 3), ("b_k_gain", 3),
     ("c_2", KD), ("c_ctx_2", KD)],
    [("norm_mix_pre_2", 2 * KD), ("norm_mix_post_2", 2 * KD), ("norm_mlp_pre_2", 2 * KD), ("norm_mlp_post_2", 2 * KD),
     ("attn_subln_2", 1), ("hy_b_in_2", 3 * KD), ("hy_b_short_2", 3 * KD), ("hy_bias_2", KD)],
    [("hy_w_short_2", 9 * KD), ("hy_b_out_2", KD)],
    [("b_mod_2", 12 * KD)],
]


def flat_rows(ap):
    shape = ap.shape
    if len(shape) == 1:
        return ap.rearrange("(r p) -> r p", p=P)
    if len(shape) == 2:
        return ap.rearrange("a (r p) -> (a r) p", p=P)
    return ap.rearrange("a b (r p) -> (a b r) p", p=P)


def build(nc, I, out):
    ctx = ExitStack()
    with ctx:
        def sem(name):
            return ctx.enter_context(nc.semaphore(name))

        def sb(name, shape, dt=F32, st=ctx):
            return st.enter_context(nc.sbuf_tensor(name, shape, dt))

        pr = Program(nc, sem)
        A, Ad, V, Vp, G, T = pr.A, pr.Adyn, pr.V, pr.Vpin, pr.G, pr.T

        x = sb("x", [P, KD, S])
        with ExitStack() as st:
            Yh, Yl = sb("Yh", [P, KD, S], F32R, st), sb("Yl", [P, KD, S], F32R, st)
        with ExitStack() as st:
            xctx = sb("xctx", [P, KD, CTX], F32, st)
            kcF = sb("kcF", [P, 2, 512], F32, st)
        sb("overY", [P, 2 * KD, S])
        Wr = sb("Wr", [P, 2, 2048])
        Wh, Wl = sb("Wh", [P, 2, 2048], F32R), sb("Wl", [P, 2, 2048], F32R)
        ones, ident = sb("ones", [P, P]), sb("ident", [P, P])
        NCOL = sum(r for pk in PACKS for _, r in pk)
        PK = sb("PK", [P, NCOL])
        mod = sb("mod", [P, 112])
        GC = sb("GC", [P, 2, 5, KD])
        sc2 = sb("sc2", [P, KD, 2])
        eps = sb("eps", [P, 2])
        acc = sb("acc", [P, S])
        rc = sb("rc", [P, 2, TT])
        rs = sb("rs", [P, 2, S])
        sq = sb("sq", [P, 2, S])
        tmp = sb("tmp", [P, 4, S])
        ps = [ctx.enter_context(nc.psum_tensor(f"ps{b}", [P, S], F32)) for b in range(4)]
        psx = ctx.enter_context(nc.psum_tensor("psx", [P, 4, S], F32))
        kspec = nc.dram_tensor("kspec", (2, TT, P, D), F32).ap()

        col = {}
        off = 0
        for pk in PACKS:
            for n, r in pk:
                col[n] = off
                off += r

        def pc(name, i):
            return PK[:, col[name] + i:col[name] + i + 1]

        def phase(*tensors):
            with ExitStack() as st:
                return [sb(n, s, d, st) for n, s, d in tensors]

        with ExitStack() as over:
            Ah, Al = sb("Ah", [P, KD, S], F32R, over), sb("Al", [P, KD, S], F32R, over)
            stage, rows = phase(("stage", [P, TT, D], F32), ("rows", [P, 4, P], F32))
            vA, wsT, bA, szA, modw, macc, ssA, vst = phase(
                ("vA", [P, TT, AW], F32), ("wsT", [P, 8, P], F32), ("bA", [P, 8, P], F32), ("szA", [P, 2, S], F32),
                ("modw", [P, 2, 2, 512], F32), ("macc", [P, 512], F32), ("ssA", [P, 16], F32), ("vst", [P, 2, S], F32))
            QB, KB, VB, maskB, PB, ropeB, onB, stB = phase(
                ("QB", [P, 3, 2, S], F32), ("KB", [P, 3, 2, S], F32), ("VB", [P, 3, TT, 256], F32),
                ("maskB", [P, 27 * P], BF16), ("PB", [P, 2304], F32), ("ropeB", [32, 2, S], F32), ("onB", [P, 2, P], F32),
                ("stB", [P, TT, 4], F32))
            xcC, s0C, s1C, Ch, Cl, szC, cntC = phase(
                ("xcC", [P, 2, S + 16], F32), ("s0C", [P, S + 16], F32), ("s1C", [P, S + 16], F32),
                ("Ch", [P, 4, S], F32R), ("Cl", [P, 4, S], F32R), ("szC", [P, 4, S], F32), ("cntC", [P, 4, S], F32))
            QD, KDt, VD, Uh, Ul, PD, ropeD, stD = phase(
                ("QD", [P, 4, S], F32), ("KDt", [P, 4, S + CTX], F32), ("VD", [P, TT + CT, 512], F32),
                ("Uh", [P, KD, CTX], F32R), ("Ul", [P, KD, CTX], F32R), ("PD", [P, 2, S + CTX], F32),
                ("ropeD", [P, 2, S], F32), ("stD", [P, 24], F32))
            yt, = phase(("yt", [P, KD, S], F32))
            x0H, wH, over1, uH = phase(("x0H", [P, KD, S], F32), ("wH", [P, KD, S], F32), ("over1", [P, 2, TT, 512], F32),
                                       ("uH", [P, 2, S + 2], F32))
            over2, hdF, kF, hsF, hdiffF = phase(
                ("over2", [P, 4, S], F32), ("hdF", [64, 2, S], F32), ("kF", [64, S], F32),
                ("hsF", [P, TT, 512], F32), ("hdiffF", [P, TT, 512], F32))
        tabF, woF, dlF, zF, w2F, w1F, colF = phase(
            ("tabF", [P, 2, TT, S], F32), ("woF", [64, 2 * D], F32), ("dlF", [P, D], F32), ("zF", [33, S], F32),
            ("w2F", [64, 2, 64], F32), ("w1F", [33, 64], F32), ("colF", [P, 16], F32))
        kS, yS, over0, tabH, wtH = phase(
            ("kS", [P, 2, TT, 512], F32), ("yS", [P, 2, TT, 512], F32), ("over0", [P, 2 * KD, S], F32),
            ("tabH", [P, 2, TT, 512], F32), ("wtH", [P, TT, 512], F32))
        kS0 = Yh[:].bitcast(F32).rearrange("p (w f) n -> p w f n", w=2)

        block = ctx.enter_context(nc.Block())
        pr.credit()

        raw = [pr.dma_counter("raw0"), pr.dma_counter("raw1")]
        pr.ctr["hi"] = Counter(sem("hi"), 1, CREDIT)
        pr.ctr["lo"] = Counter(sem("lo"), 1, CREDIT)
        pr.ctr["panels"] = Counter(None, 1, CREDIT)
        nc.scalar.sem_inc(pr.ctr["hi"].sem, CREDIT)
        nc.gpsimd.sem_inc(pr.ctr["lo"].sem, CREDIT)
        state = {"n": 0}

        def split_done(behind):
            c = pr.ctr["panels"]
            return Mark(pr.ctr["lo"], c.const, tuple(pr.loops), back=behind)

        def load_panel(src):
            s = state["n"] % 2
            state["n"] += 1
            pr.wait("sp", split_done(1))
            pr.pin("sp")
            pr.emit("sp", lambda e: e.dma_start(Wr[:, s, :].rearrange("p (k n) -> p k n", k=src.shape[1]), src), ctr=raw[s])
            pr.ctr["panels"].const += 1
            return s

        def split_panel(s):
            c = pr.ctr[raw[s]]
            pr.wait("act", Mark(c, c.const, tuple(pr.loops), back=-16), "pe_slot%d" % s)
            mh = pr.emit("act", lambda e: e.activation(Wh[:, s, :], Wr[:, s, :], ACT.Copy), ctr="hi")
            pr.wait("pool", mh)
            pr.emit("pool", lambda e: e.tensor_tensor(Wl[:, s, :], Wr[:, s, :], Wh[:, s, :].bitcast(F32), ALU.subtract), ctr="lo")

        def panel(src, tiles, epis, more=True, pre=None, mid=None):
            s = load_panel(src)
            if more:
                split_panel(1 - s)
            if pre:
                pre()
            pr.wait("pe", split_done(0))
            for n, (tile, epi) in enumerate(zip(tiles, epis)):
                m = tile(s)
                if n == len(tiles) - 1:
                    pr.name("pe_slot%d" % s, m)
                epi(m)
                if mid and n == 0:
                    mid()

        def mm3(o, ah, al, bh, bl, first, last):
            pr.raw("pe", lambda e: e.matmul(o, ah, bh, start=first, stop=False))
            pr.raw("pe", lambda e: e.matmul(o, ah, bl, start=False, stop=False))
            return lambda e: e.matmul(o, al, bh, start=False, stop=last)

        def wpart(W, s, k, c0, c1, kt=KD):
            return W[:, s, :].rearrange("p (k n) -> p k n", k=kt)[:, k, c0:c1]

        def tile_F(n, hi, lo, bank, ready=None, kt=KD, cols=S):
            def go(s):
                pr.wait("pe", "rel%d" % bank)
                m = None
                for k in range(kt):
                    if ready:
                        pr.wait("pe", ready(k))
                    f = mm3(ps[bank][:, 0:cols], wpart(Wh, s, k, n * P, n * P + P, kt), wpart(Wl, s, k, n * P, n * P + P, kt),
                            hi[:, k, :], lo[:, k, :], k == 0, k == kt - 1)
                    if k < kt - 1:
                        pr.raw("pe", f)
                    else:
                        m = pr.emit("pe", f)
                return m
            return go

        def tile_T(pair, hi, lo, bank, ready=None):
            def go(s):
                pr.wait("pe", "rel%d" % bank)
                m = None
                for j, t in enumerate(pair):
                    for k in range(KD):
                        if ready:
                            pr.wait("pe", ready(k))
                        f = mm3(ps[bank][:, j * 256:(j + 1) * 256], hi[:, k, t * P:(t + 1) * P], lo[:, k, t * P:(t + 1) * P],
                                wpart(Wh, s, k, 0, 256), wpart(Wl, s, k, 0, 256), k == 0, k == KD - 1)
                        if k < KD - 1 or t != pair[-1]:
                            pr.raw("pe", f)
                        else:
                            m = pr.emit("pe", f)
                return m
            return go

        CARRY = [("pe", "rel0", "rel1", "rel2", "rel3"), ("act", "pe_slot0", "pe_slot1")]

        def ksrc(w, k0, n0):
            return w.rearrange("(k p) n -> p k n", p=P)[:, bass.ds(k0, KD), bass.ds(n0, 256)]

        def now(e):
            c = pr.ctr[e]
            return Mark(c, c.const, tuple(pr.loops))

        def new_phase(*more):
            for e in ("act", "dve", "pe", "pool") + more:
                pr.wait(e, now("act"), now("dve"), now("pe"), now("pool"), now("norm_act"), now("norm_dve"), now("norm_pool"))

        def rms_sum(src, o, *waits, cols=S, name=None):
            pr.wait("pe", *waits)
            for t in range(cols // P):
                fn = lambda e: e.matmul(o[:, t:t + 1], src[:, t * P:(t + 1) * P], ones[:, 0:1], start=True, stop=True)
                if t < cols // P - 1:
                    pr.raw("pe", fn)
                else:
                    return T(fn, name=name)

        def square_sum(k, *waits, cols=S):
            return T(lambda e: e.matmul(psx[:, 2, 0:cols], ones[:], sq[:, k % 2, 0:cols], start=(k == 0), stop=(k == KD - 1)),
                     *waits, name="sqr%d" % (k % 2))

        def rms_inverse(m, n_feat, o, r=0, cols=S):
            n = cols // P
            m = A(lambda e: e.activation(rc[:, r, 0:n], o[:, 0:n], ACT.Sqrt, bias=eps[:, 0:1], scale=1.0 / n_feat),
                  m, "rc%d" % r)
            return V(lambda e: e.reciprocal(rc[:, r, 0:n], rc[:, r, 0:n]), m)

        def rms_spread(m, o, *waits, r=0, cols=S):
            pr.wait("pe", m, *waits)
            for t in range(cols // P):
                m = T(lambda e: e.matmul(o[:, t * P:(t + 1) * P], rc[:, r, t:t + 1].to_broadcast([P, P]), ident[:],
                                         start=True, stop=True), name="rc%d" % r)
            return m

        pr.dma_counter("ldc")
        pr.dma_counter("ldi")
        pr.dma_counter("ldx")
        ml = None
        for b in range(TT):
            ml = pr.emit("sp", lambda e: e.dma_start(stage[:, b, :], I["x"][0, b * P:(b + 1) * P, :]), ctr="ldx")
        m_x = ml
        m_id = pr.emit("act", lambda e: e.dma_start(ident[:], I["k_ident"]), ctr="ldi")
        for n, pk in enumerate(PACKS):
            r = 0
            for name, cnt in pk:
                ml = pr.emit("act", lambda e: e.dma_start(rows[r:r + cnt, n, :], flat_rows(I[name])), ctr="ldc")
                r += cnt
        m_c = ml
        V(lambda e: e.memset(ones[:], 1.0), name="ones")
        V(lambda e: e.memset(eps[:], EPS))
        V(lambda e: e.memset(acc[:], 0.0), name="acc")
        split_panel(0)
        pr.wait("pe", m_x, m_id, "ones")
        for k in range(KD):
            b = k % 4
            pr.wait("pe", "rel%d" % b)
            for t in range(TT):
                m = T(lambda e: e.transpose(ps[b][:, t * P:(t + 1) * P], stage[:, t, k * P:(k + 1) * P], ident[:]))
            mx = V(lambda e: e.tensor_copy(x[:, k, :], ps[b][:]), m, name="rel%d" % b)
            ms = A(lambda e: e.activation(sq[:, k % 2, :], x[:, k, :], ACT.Square), mx, "sqr%d" % (k % 2))
            if k:
                square_sum(k - 1, m_sq)
            m_sq = ms
        summed0 = square_sum(KD - 1, m_sq)
        pr.wait("pe", m_c)
        off = 0
        for n, pk in enumerate(PACKS):
            r = sum(c for _, c in pk)
            m = T(lambda e: e.transpose(psx[:, 0, off:off + r], rows[0:r, n, :], ident[0:r, 0:r]))
            off += r
        m = V(lambda e: e.tensor_copy(PK[:], psx[:, 0, 0:NCOL]), m, name="PK")
        pr.name("relx0", m)
        m = A(lambda e: e.activation(sc2[:, :, 0], PK[:, col["c_2"]:col["c_2"] + KD], ACT.Silu), "PK")
        A(lambda e: e.activation(sc2[:, :, 1], PK[:, col["c_ctx_2"]:col["c_ctx_2"] + KD], ACT.Silu), name="sc2")

        def norm(gain, bias=None, srcx=x, hi=Ah, lo=Al, free="h_free", cols=S, tag="h", summed=None):
            def on(e, fn, *waits):
                pr.wait(e, *waits)
                return pr.emit(e, fn, ctr="norm_" + e)
            if summed is None:
                m = rms_inverse(rms_sum(acc, psx[:, 2, :], "acc", "relx2", cols=cols, name="acc_read"), D, psx[:, 2, :], cols=cols)
                pr.name("relx2", m)
                m = rms_spread(m, psx[:, 3, :], "relx3", cols=cols)
                r, free_r = psx[:, 3, 0:cols], "relx3"
            else:
                r, free_r = rs[:, 0, 0:cols], "rsr0"
                m = A(lambda e: e.activation(r, psx[:, 2, 0:cols], ACT.Sqrt, bias=eps[:, 0:1], scale=1.0 / D), summed, free_r, name="relx2")
                m = V(lambda e: e.reciprocal(r, r), m)
            for e in ("act", "dve", "pool"):
                pr.wait(e, free)
            pend = []

            def fin(k, mh):
                t, h = tmp[:, k % 4, 0:cols], hi[:, k, :].bitcast(F32)
                m = on("pool" if k % 2 else "dve", lambda e: e.tensor_tensor(lo[:, k, :], t, h, ALU.subtract), mh)
                pr.name("%s%d" % (tag, k), m)
                pr.name("tmp%d" % (k % 4), m)
            for k in range(KD):
                t = tmp[:, k % 4, 0:cols]
                mt = on("dve", lambda e: e.scalar_tensor_tensor(t, srcx[:, k, :], gain(k), r, ALU.mult, ALU.mult), m, "tmp%d" % (k % 4))
                if k == KD - 1:
                    pr.name(free_r, mt)
                if bias:
                    on("act", lambda e: e.activation(hi[:, k, :], t, ACT.Identity, bias=bias(k)), mt)
                    mh = on("act", lambda e: e.activation(t, t, ACT.Identity, bias=bias(k)))
                else:
                    mh = on("act", lambda e: e.activation(hi[:, k, :], t, ACT.Copy), mt)
                pend.append((k, mh))
                if len(pend) > 1:
                    fin(*pend.pop(0))
            while pend:
                fin(*pend.pop(0))

        def y_ready(k):
            return "y%d" % k

        def h_ready(k):
            return "h%d" % k

        def out_product(w, k0, final, hi=Yh, lo=Yl, last_panels=False):
            if final:
                V(lambda e: e.memset(acc[:], 0.0), "acc_read", name="accw")

            def body(i, last=False):
                def epi(b):
                    def go(m):
                        n = i * 4 + b
                        mx = V(lambda e: e.tensor_tensor(x[:, bass.ds(n, 1), :], x[:, bass.ds(n, 1), :],
                                                         ps[b][:].rearrange("p (a n) -> p a n", a=1), ALU.add),
                               m, name="rel%d" % b)
                        if final:
                            ms = Ad(lambda e: e.activation(sq[:, b % 2, :].rearrange("p (a n) -> p a n", a=1),
                                                           x[:, bass.ds(n, 1), :], ACT.Square), mx, "sqr%d" % (b % 2))
                            V(lambda e: e.tensor_tensor(acc[:], acc[:], sq[:, b % 2, :], ALU.add), ms, "accw", name="accw")
                            pr.name("sqr%d" % (b % 2), pr.names["accw"])
                    return go
                for j in range(2):
                    panel(ksrc(w, k0, i * 512 + j * 256),
                          [tile_F(0, hi, lo, 2 * j, y_ready), tile_F(1, hi, lo, 2 * j + 1, y_ready)],
                          [epi(2 * j), epi(2 * j + 1)])
            pr.loop(2, body, carry=CARRY + [("act", "sqr0", "sqr1"), ("dve", "accw")])
            pr.name("y_free", now("pe"))
            if final:
                pr.name("acc", pr.last("accw"))

        pr.dma_counter("modw0")
        pr.dma_counter("modw1")

        def mod_load(layer, nb, kp):
            src = I["w_mod_2"][layer].rearrange("(k p) n -> p k n", p=P)[:, 2 * kp:2 * kp + 2, bass.ds(nb * 512, 512)]
            pr.wait("act", "modr%d" % (kp % 2))
            pr.emit("act", lambda e: e.dma_start(modw[:, kp % 2, :, :], src), ctr="modw%d" % (kp % 2), name="modl%d" % (kp % 2))

        def mod_use(kp, accs):
            for r in range(2):
                k = 2 * kp + r
                for who, t, nm in accs:
                    w = modw[:, kp % 2, r, :]
                    if k == 0:
                        m = V(lambda e: e.tensor_scalar(t, w, sc2[:, k, who:who + 1], None, ALU.mult), "modl0", "sc2", nm, name=nm)
                    else:
                        m = V(lambda e: e.scalar_tensor_tensor(t, w, sc2[:, k, who:who + 1], t, ALU.mult, ALU.add),
                              "modl%d" % (kp % 2), nm, name=nm)
            pr.name("modr%d" % (kp % 2), m)

        def mod_sum(nb, accs):
            pr.wait("pe", *[nm for _, _, nm in accs])
            pr.pin("pe")
            for who, t, nm in accs:
                for r in range(4):
                    m = T(lambda e: e.matmul(psx[:, 1, bass.ds(nb * 4 + (64 * who + r), 1)], t[:, r * P:(r + 1) * P], ones[:, 0:1],
                                             start=True, stop=True))
                pr.name(nm, m)
            pr.name("modsum", m)

        pr.dma_counter("lda")

        def mixer_a(layer, j, summed=None, load_ahead=None):
            win, wout = I["a_w_in"][j], I["a_w_out"][j]
            wsr = vst[:].rearrange("p a n -> p (a n)").rearrange("p (g n) -> p g n", g=8)
            new_phase()
            m_ws = pr.emit("act", lambda e: e.dma_start(wsr, I["a_w_s"][j].rearrange("g i j -> i g j")), ctr="lda")
            m_ws = pr.emit("act", lambda e: e.dma_start(bA[:].rearrange("p g n -> p (g n)"),
                                                        I["a_b_s"][j].rearrange("g i -> (g i)").partition_broadcast(P)), ctr="lda")
            norm(lambda k: pc("norm_gain", layer * KD + k), free="h_free", summed=summed)
            m_cm = G(lambda e: e.affine_select(out=wsr, in_=wsr, compare_op=ALU.is_ge, fill=0.0, base=0,
                                               pattern=[[0, 8], [-1, P]], channel_multiplier=1), m_ws)
            V(lambda e: e.memset(ssA[:, 0:4], 0.0), name="ssA")
            pr.wait("pe", "sc2", "relx1")
            pr.wait("dve", m_ws)

            def v_body(i):
                def epi(q, pair, b):
                    def go(m):
                        for jj, t in enumerate(pair):
                            A(lambda e: e.activation(sq[:, jj, 0:256], ps[b][:, jj * 256:(jj + 1) * 256], ACT.Square,
                                                     accum_out=ssA[:, 4 + 4 * q + t:5 + 4 * q + t]),
                              m, "ssr%d" % q, "sqa%d" % jj, name="sqa%d" % jj)
                        for jj, t in enumerate(pair):
                            mv = V(lambda e: e.tensor_scalar(vA[:, t, bass.ds(i * 512 + q * 256, 256)],
                                                             ps[b][:, jj * 256:(jj + 1) * 256], 1.0, None, ALU.mult), "sqa1")
                        pr.name("rel%d" % b, mv)
                        if b % 2:
                            V(lambda e: e.tensor_tensor(ssA[:, 0:4], ssA[:, 0:4], ssA[:, 4 + 4 * q:8 + 4 * q], ALU.add),
                              "sqa1", "ssA", name="ssA")
                            pr.name("ssr%d" % q, pr.names["ssA"])
                    return go
                accs = [(0, macc[:], "mac0")] + ([(1, szA[:, 0, :], "mac1")] if j == 0 else [])

                def use(q):
                    mod_use(2 * q, accs)
                    mod_use(2 * q + 1, accs)
                for q in range(2):
                    panel(ksrc(win, 0, AW + i * 512 + q * 256),
                          [tile_T((0, 1), Ah, Al, 2 * q, h_ready), tile_T((2, 3), Ah, Al, 2 * q + 1, h_ready)],
                          [epi(q, (0, 1), 2 * q), epi(q, (2, 3), 2 * q + 1)],
                          pre=lambda: (mod_load(j, i, 2 * q), mod_load(j, i, 2 * q + 1), q and use(q)),
                          mid=lambda: q or use(q))
                mod_sum(i, accs)
            carry_mod = [("act", "modr0", "modr1"), ("dve", "mac0", "mac1")]
            pr.loop(4, v_body, carry=CARRY + carry_mod + [("act", "ssr0", "ssr1", "sqa0", "sqa1"), ("dve", "ssA")])
            pr.wait("pe", m_cm)
            for g in range(8):
                b = 2 + g // 4
                pr.wait("pe", "relx%d" % b)
                m = T(lambda e: e.transpose(psx[:, b, (g % 4) * P:(g % 4) * P + P], wsr[:, g, :], ident[:]))
                if g % 4 == 3:
                    m = V(lambda e: e.tensor_copy(wsT[:, g - 3:g + 1, :].rearrange("p g n -> p (g n)"), psx[:, b, :]), m,
                          name="relx%d" % b)
            pr.name("vst0", m)
            pr.name("vst1", m)
            m = A(lambda e: e.activation(ssA[:, 12:16], ssA[:, 0:4], ACT.Sqrt, bias=eps[:, 0:1], scale=1.0 / AW), "ssA")
            m_rv = V(lambda e: e.reciprocal(ssA[:, 12:16], ssA[:, 12:16]), m)
            rv = ssA[:, 12:16]

            for half in range(2):
                def body(i):
                    def epi_z(f):
                        def go(m):
                            A(lambda e: e.activation(szA[:, f, :], ps[f][:], ACT.Silu), m, "szr%d" % f, name="rel%d" % f)
                        return go

                    def epi_u(f):
                        def go(m):
                            pr.name("ut%d" % f, m)
                        return go
                    q = i + half * 4
                    accs = [(0, macc[:], "mac0")]
                    for f in range(2):
                        vt = V(lambda e: e.tensor_tensor(vst[:, f, :].rearrange("p (t n) -> p t n", t=TT),
                                                         vA[:, :, bass.ds(q * 256 + f * P, P)],
                                                         rv.rearrange("p (t a) -> p t a", a=1).to_broadcast([P, TT, P]), ALU.mult),
                               m_rv, "vst%d" % f, name="vsw%d" % f)
                    panel(ksrc(win, 0, 2 * AW + q * 256), [tile_F(0, Ah, Al, 0), tile_F(1, Ah, Al, 1)], [epi_z(0), epi_z(1)],
                          pre=lambda: (mod_load(j, q + 4, 0), mod_load(j, q + 4, 1)),
                          mid=lambda: (mod_use(0, accs), mod_use(1, accs)))
                    for f in range(2):
                        pr.wait("pe", "vsw%d" % f, "relx%d" % (2 * f))
                        pr.pin("pe")
                        for t in range(TT):
                            fn = lambda e: e.matmul(psx[:, 2 * f, t * P:(t + 1) * P], vst[:, f, t * P:(t + 1) * P],
                                                    wsT[:, bass.ds(q, 1), :].rearrange("p a n -> p (a n)"), start=True, stop=True)
                            if t < TT - 1:
                                pr.raw("pe", fn)
                            else:
                                T(fn, name="vst%d" % f)
                    m_mix = [pr.names["vst0"], pr.names["vst1"]]
                    panel(ksrc(win, 0, q * 256), [tile_F(0, Ah, Al, 2), tile_F(1, Ah, Al, 3)], [epi_u(0), epi_u(1)],
                          pre=lambda: (mod_load(j, q + 4, 2), mod_load(j, q + 4, 3)),
                          mid=lambda: (mod_use(2, accs), mod_use(3, accs)))
                    mod_sum(q + 4, accs)
                    pend = []
                    for f in range(2):
                        gcol = PK[:, bass.ds(col["a_v_gain"] + j * 16 + q * 2 + f, 1)]
                        bb = bA[:, bass.ds(q, 1), :].to_broadcast([P, TT, P])
                        y = tmp[:, f, :]
                        y3 = y.rearrange("p (t n) -> p t n", t=TT)
                        m = V(lambda e: e.scalar_tensor_tensor(y3, psx[:, 2 * f, :].rearrange("p (t n) -> p t n", t=TT), gcol, bb,
                                                               ALU.mult, ALU.add), m_mix[f], "tmp%d" % f, name="relx%d" % (2 * f))
                        m = V(lambda e: e.tensor_tensor(y, y, szA[:, f, :], ALU.mult), m, "rel%d" % f, name="szr%d" % f)
                        m = V(lambda e: e.tensor_tensor(y, y, ps[2 + f][:], ALU.mult), m, "ut%d" % f, name="rel%d" % (2 + f))
                        mh = Ad(lambda e: e.activation(Yh[:, bass.ds(i * 2 + f, 1), :], y.rearrange("p (a n) -> p a n", a=1), ACT.Copy), m)
                        pend.append((f, mh))
                    for f, mh in pend:
                        y = tmp[:, f, :].rearrange("p (a n) -> p a n", a=1)
                        V(lambda e: e.tensor_tensor(Yl[:, bass.ds(i * 2 + f, 1), :], y, Yh[:, bass.ds(i * 2 + f, 1), :].bitcast(F32),
                                                    ALU.subtract), mh, name="tmp%d" % f)
                pr.wait("act", "y_free")
                pr.wait("dve", "y_free")
                pr.loop(4, body, carry=CARRY + carry_mod + [("act", "szr0", "szr1"), ("dve", "vst0", "vst1", "tmp0", "tmp1"),
                                                            ("pe", "relx0", "relx2")])
                for k in range(KD):
                    pr.name("y%d" % k, now("dve"))
                pr.name("h_free", now("pe"))
                if half and load_ahead:
                    load_ahead()
                out_product(wout, half * KD, half == 1)
            bc = col["b_mod_2"] + 48 * j
            V(lambda e: e.tensor_tensor(mod[:, 48 * j:48 * j + 48], psx[:, 1, 0:48], PK[:, bc:bc + 48], ALU.add), "modsum", name="relx1")
            if j == 0:
                V(lambda e: e.tensor_tensor(mod[:, 96:112], psx[:, 1, 64:80], PK[:, bc:bc + 16], ALU.add), name="relx1")

        def split_tile(src, m, k, hi=None, lo=None, dyn=False, slot=None, name=None):
            hi = Yh if hi is None else hi
            lo = Yl if lo is None else lo
            s3 = src.rearrange("p (a n) -> p a n", a=1)
            mh = (Ad if dyn else A)(lambda e: e.activation(hi[:, bass.ds(k, 1), :], s3, ACT.Copy), m)
            m = V(lambda e: e.tensor_tensor(lo[:, bass.ds(k, 1), :], s3, hi[:, bass.ds(k, 1), :].bitcast(F32), ALU.subtract), mh)
            if slot:
                pr.name(slot, m)
            if name:
                pr.name(name, m)
            return m

        swap = [(i + 16) % 32 for i in range(32)]

        def rope(q, cs, m, t=tmp[:, 3, :], name="tmp3", add=V):
            t = t[0:q.shape[0], :]
            m1 = Vp(lambda e: e.stream_shuffle(t, q, swap), m, name)
            m2 = V(lambda e: e.tensor_tensor(t, t, cs[:, 1, :], ALU.mult), m1)
            m3 = V(lambda e: e.tensor_tensor(q, q, cs[:, 0, :], ALU.mult), m1)
            return add(lambda e: e.tensor_tensor(q, q, t, ALU.add), m2, m3, name=name)

        pr.dma_counter("ldb")
        psf = psx[:].rearrange("p b n -> p (b n)")
        tmpf = tmp[:].rearrange("p b n -> p (b n)")
        NB = [min(2, j + 1) + 2 * (j + 1) for j in range(TT)]
        MOFF = [sum(NB[:j]) * P for j in range(TT)]

        def blocks(j):
            return [(0, t) for t in range(max(0, j - 1), j + 1)] + [(g, t) for g in (1, 2) for t in range(j + 1)]

        def mixer_b():
            win, wout = I["b_w_in"][0], I["b_w_out"][0]
            new_phase()
            HM = 27 * P // 2
            qf = QB[:].rearrange("p a b n -> p (a b n)")
            pr.emit("act", lambda e: e.dma_start(PB[:, 0:HM], I["k_maskB"][:, 0:HM]), ctr="ldb")
            pr.emit("act", lambda e: e.dma_start(qf[:, 0:HM], I["k_maskB"][:, HM:2 * HM]), ctr="ldb")
            m_mask = pr.emit("act", lambda e: e.dma_start(ropeB[:], I["k_ropeB"]), ctr="ldb")
            norm(lambda k: pc("norm_gain", KD + k), free="h_free")
            V(lambda e: e.tensor_copy(maskB[:, 0:HM], PB[:, 0:HM]), m_mask)
            m = V(lambda e: e.tensor_copy(maskB[:, HM:2 * HM], qf[:, 0:HM]))
            pr.name("mask", m)
            pr.wait("dve", m)
            scale = 1.0 / float(np.sqrt(P))

            def body(i):
                cnt = [0]
                pend = []

                def flush():
                    while pend:
                        pend.pop(0)()

                def epi_qk(dst, gain, b):
                    def go(m):
                        flush()
                        t = cnt[0]
                        cnt[0] += 1
                        r, c3, bank = t % 2, t % 3, 2 + t % 2
                        ms = A(lambda e: e.activation(sq[:, r, :], ps[b][:], ACT.Square), m, "sqr%d" % r)
                        mc = A(lambda e: e.activation(tmp[:, c3, :], ps[b][:], ACT.Copy), "tmp%d" % c3, name="rel%d" % b)

                        def rest():
                            m = T(lambda e: e.matmul(psx[:, bank, :], ones[:], sq[:, r, :], start=True, stop=True),
                                  ms, "relx%d" % bank, name="sqr%d" % r)
                            m = A(lambda e: e.activation(rs[:, r, :], psx[:, bank, :], ACT.Sqrt, bias=eps[:, 0:1], scale=1.0 / P),
                                  m, "rsr%d" % r, name="relx%d" % bank)
                            m = V(lambda e: e.reciprocal(rs[:, r, :], rs[:, r, :]), m)
                            m = V(lambda e: e.scalar_tensor_tensor(dst, tmp[:, c3, :], gain, rs[:, r, :], ALU.mult, ALU.mult),
                                  m, mc, "qk_free", name="tmp%d" % c3)
                            pr.name("rsr%d" % r, m)
                            spare, name = ((tmp[:, 3, :], "tmp3"), (acc[:], "acc_rope"))[r]
                            rope(dst[0:32, :], ropeB, m, spare, name, add=G)
                        pend.append(rest)
                    return go

                def epi_v(g, pair, b):
                    def go(m):
                        flush()
                        V(lambda e: e.tensor_copy(VB[:, g, pair[0]:pair[0] + 2, :], ps[b][:].rearrange("p (t n) -> p t n", t=2)),
                          m, "qk_free", name="rel%d" % b)
                    return go

                def epi_z(f, b):
                    def go(m):
                        A(lambda e: e.activation(sq[:, f, :], ps[b][:], ACT.Silu), m, "sqr%d" % f, name="rel%d" % b)
                        pr.name("z%d" % f, pr.names["rel%d" % b])
                    return go
                nb = 0
                for g in range(3):
                    for qk, dst in ((0, QB), (1, KB)):
                        b = nb % 4
                        nb += 2
                        gn = pc("b_q_gain" if qk == 0 else "b_k_gain", g)
                        ready = h_ready if g == 0 and qk == 0 else None
                        panel(ksrc(win, 0, (qk * 3 + g) * D + i * 256), [tile_F(0, Ah, Al, b, ready), tile_F(1, Ah, Al, b + 1)],
                              [epi_qk(dst[:, g, 0, :], gn, b), epi_qk(dst[:, g, 1, :], gn, b + 1)])
                for g in range(3):
                    b = nb % 4
                    nb += 2
                    panel(ksrc(win, 0, (6 + g) * D + i * 256), [tile_T((0, 1), Ah, Al, b), tile_T((2, 3), Ah, Al, b + 1)],
                          [epi_v(g, (0, 1), b), epi_v(g, (2, 3), b + 1)])
                qk_done = (now("dve"), now("pool"))

                def scores(hh, j):
                    W, u, v = NB[j] * P, j % 2, j
                    po = 0 if u == 0 else 1024
                    pr.wait("pe", *qk_done, "relx0", "relx1", "relx2")
                    runs = []
                    for pos, (g, t) in enumerate(blocks(j)):
                        if runs and runs[-1][1] == g and pos % 4:
                            runs[-1][3] += 1
                        else:
                            runs.append([pos, g, t, 1])
                    for n, (pos, g, t, c) in enumerate(runs):
                        fn = lambda e: e.matmul(psf[:, pos * P:(pos + c) * P], QB[:, g, hh, j * P:(j + 1) * P],
                                                KB[:, g, hh, t * P:(t + c) * P], start=True, stop=True)
                        if n < len(runs) - 1:
                            pr.raw("pe", fn)
                        else:
                            m = T(fn)
                    m = Vp(lambda e: e.tensor_tensor_reduce(PB[:, po:po + W], psf[:, 0:W], maskB[:, MOFF[j]:MOFF[j] + W], 1.0, 10 * NEG,
                                                           ALU.add, ALU.max, stB[:, v, 0:1]), m, "pb%d" % u, "st%d" % v, name="relx0")
                    pr.name("relx1", m)
                    pr.name("relx2", m)
                    m = V(lambda e: e.tensor_scalar(stB[:, v, 1:2], stB[:, v, 0:1], -scale, None, ALU.mult), m)
                    m = A(lambda e: e.activation(PB[:, po:po + W], PB[:, po:po + W], ACT.Exp, bias=stB[:, v, 1:2], scale=scale,
                                                 accum_out=stB[:, v, 2:3]), m)
                    mr = V(lambda e: e.reciprocal(stB[:, v, 3:4], stB[:, v, 2:3]), m)
                    return m, mr

                units = [(hh, j) for hh in range(2) for j in range(TT)]
                groups = [(u, q0) for u, (hh, j) in enumerate(units) for q0 in range(0, NB[j], 4)]
                done, evs, later = {}, {}, []
                turn = [(psx[:, 3, :], "relx3"), (ps[2][:], "rel2"), (ps[3][:], "rel3")]

                def flip(n):
                    u, q0 = groups[n]
                    hh, j = units[u]
                    po, w, c = (0 if j % 2 == 0 else 1024) + q0 * P, min(4, NB[j] - q0), n % 4
                    tb, nm = turn[n % 3]
                    pr.wait("pe", done[u][0], nm)
                    for r in range(w):
                        m = T(lambda e: e.transpose(tb[:, r * P:(r + 1) * P], PB[:, po + r * P:po + (r + 1) * P], ident[:]))
                    pr.name("pb%d" % (j % 2), m)
                    if n % 2 == 0:
                        evs[n] = V(lambda e: e.tensor_copy(tmp[:, c, 0:w * P], tb[:, 0:w * P]), m, "tmp%d" % c, name=nm)
                    else:
                        evs[n] = A(lambda e: e.activation(tmp[:, c, 0:w * P], tb[:, 0:w * P], ACT.Copy), m, "tmp%d" % c, name=nm)

                def values(n):
                    u, q0 = groups[n]
                    hh, j = units[u]
                    bl = blocks(j)
                    pr.wait("pe", evs[n], "rel0")
                    for pos in range(q0, min(q0 + 4, len(bl))):
                        g, t = bl[pos]
                        m = T(lambda e: e.matmul(ps[0][:, j * P:(j + 1) * P], tmp[:, n % 4, (pos % 4) * P:(pos % 4 + 1) * P],
                                                 VB[:, g, t, hh * P:(hh + 1) * P], start=(pos == 0), stop=(pos == len(bl) - 1)),
                              name="tmp%d" % (n % 4))
                    if q0 + 4 < len(bl):
                        return
                    m = V(lambda e: e.tensor_scalar(onB[:, j % 2, :], ps[0][:, j * P:(j + 1) * P], stB[:, j, 3:4], None, ALU.mult),
                          m, done[u][1], "on%d" % (j % 2), name="rel0")
                    pr.name("st%d" % j, m)

                    def back():
                        m2 = T(lambda e: e.transpose(ps[1][:, j * P:(j + 1) * P], onB[:, j % 2, :], ident[:]), m, "rel1", name="on%d" % (j % 2))
                        if j == TT - 1:
                            y = rs[:, hh, :]
                            m2 = V(lambda e: e.tensor_tensor(y, ps[1][:], sq[:, hh, :], ALU.mult), m2, "z%d" % hh, "rsr%d" % hh, name="rel1")
                            pr.name("sqr%d" % hh, m2)
                            split_tile(y, m2, i * 2 + hh, dyn=True, slot="rsr%d" % hh)
                    later.append(back)

                done[0] = scores(*units[0])
                b = nb % 4
                panel(ksrc(win, 0, 9 * D + i * 256), [tile_F(0, Ah, Al, b), tile_F(1, Ah, Al, b + 1)],
                      [epi_z(0, b), epi_z(1, b + 1)])
                for n in range(len(groups) + 2):
                    if n < len(groups):
                        u, q0 = groups[n]
                        if q0 == 0 and u + 1 < len(units):
                            done[u + 1] = scores(*units[u + 1])
                        flip(n)
                    ready, later[:] = list(later), []
                    if n >= 2:
                        values(n - 2)
                    for f in ready:
                        f()
                for f in later:
                    f()
                pr.name("qk_free", now("pe"))
            pr.loop(4, body, carry=CARRY + [("act", "sqr0", "sqr1", "tmp0", "tmp1", "tmp2", "rsr0", "rsr1"), ("pe", "relx0", "relx1", "relx2", "relx3"),
                                            ("dve", "tmp0", "tmp1", "tmp2", "tmp3", "acc_rope", "acc_read", "y_free"), ("act", "y_free")])
            pr.name("acc_read", pr.last("acc_rope"))
            for k in range(KD):
                pr.name("y%d" % k, now("dve"))
            pr.name("h_free", now("pe"))
            out_product(wout, 0, True)

        pr.dma_counter("ldcc")

        def mixer_c():
            win, wout = I["c_w_in"][0], I["c_w_out"][0]
            new_phase()
            mc = pr.emit("act", lambda e: e.dma_start(cntC[:].rearrange("p g n -> p (g n)"),
                                                      I["k_cnt"].rearrange("g n -> (g n)").partition_broadcast(P)), ctr="ldcc")
            for t in (xcC[:, 0, 0:16], xcC[:, 1, 0:16], s0C[:, 0:16], s1C[:, 0:16]):
                mz = V(lambda e: e.memset(t, 0.0))
            norm(lambda k: pc("norm_gain", 2 * KD + k), free="h_free")
            pr.wait("dve", mc, mz)
            for g in range(4):
                def epi_x(n, b):
                    def go(m):
                        r = n % 2
                        m = A(lambda e: e.activation(xcC[:, r, 16:], ps[b][:], ACT.Copy), m, "xcr%d" % r, name="rel%d" % b)
                        src = xcC[:, r, :]
                        for step in range(g + 1):
                            dst = (s0C, s1C)[step % 2]
                            sh = 1 << step
                            m = V(lambda e: e.tensor_tensor(dst[:, 16:], src[:, 16:], src[:, 16 - sh:16 + S - sh], ALU.add), m)
                            src = dst
                        m = V(lambda e: e.tensor_tensor(tmp[:, n, :], src[:, 16:], cntC[:, g, :], ALU.mult), m, "tmp%d" % n)
                        m = V(lambda e: e.tensor_tensor(tmp[:, n, :], tmp[:, n, :], xcC[:, r, 16:], ALU.subtract), m, name="xcr%d" % r)
                        pr.wait("act", "c_free")
                        pr.wait("dve", "c_free")
                        split_tile(tmp[:, n, :], m, n, Ch, Cl, slot="tmp%d" % n, name="c%d" % n)
                    return go

                def epi_z(n, b):
                    def go(m):
                        A(lambda e: e.activation(szC[:, n, :], ps[b][:], ACT.Silu), m, "szr%d" % n, name="rel%d" % b)
                        pr.name("z%d" % n, pr.names["rel%d" % b])
                    return go

                def epi_y(n, b):
                    def go(m):
                        m = V(lambda e: e.scalar_tensor_tensor(tmp[:, n, :], ps[b][:], pc("c_scale", 4 * g + n), szC[:, n, :],
                                                               ALU.mult, ALU.mult), m, "z%d" % n, "tmp%d" % n, name="rel%d" % b)
                        pr.name("szr%d" % n, m)
                        pr.wait("act", "y_free")
                        pr.wait("dve", "y_free")
                        split_tile(tmp[:, n, :], m, (g % 2) * 4 + n, slot="tmp%d" % n, name="y%d" % ((g % 2) * 4 + n))
                    return go
                for part, epi in ((0, epi_x), (AW, epi_z)):
                    for j in range(2):
                        panel(ksrc(win, 0, part + g * 512 + j * 256), [tile_F(0, Ah, Al, 2 * j, h_ready), tile_F(1, Ah, Al, 2 * j + 1, h_ready)],
                              [epi(2 * j, 2 * j), epi(2 * j + 1, 2 * j + 1)])
                pr.name("h_free", now("pe"))
                panel(I["c_w_grp"][0][g].rearrange("(k p) n -> p k n", p=P),
                      [tile_F(n, Ch, Cl, n, lambda k: "c%d" % k, kt=4) for n in range(4)], [epi_y(n, n) for n in range(4)])
                pr.name("c_free", now("pe"))
                if g % 2:
                    out_product(wout, (g // 2) * KD, g == 3)

        def product_to_yt(w, k0, bias=None, add=False, squares=False, loops=True, more=True):
            if squares:
                V(lambda e: e.memset(acc[:], 0.0), "acc_read", name="accw")

            def body(i, more=True):
                def epi(b):
                    def go(m):
                        n = i * 4 + b
                        p3 = ps[b][:].rearrange("p (a n) -> p a n", a=1)
                        if add:
                            mx = V(lambda e: e.tensor_tensor(yt[:, bass.ds(n, 1), :], yt[:, bass.ds(n, 1), :], p3, ALU.add), m, "ytw", name="rel%d" % b)
                        elif bias:
                            mx = V(lambda e: e.tensor_scalar(yt[:, bass.ds(n, 1), :], p3, PK[:, bass.ds(col[bias] + n, 1)], None, ALU.add),
                                   m, name="rel%d" % b)
                        else:
                            mx = V(lambda e: e.tensor_scalar(yt[:, bass.ds(n, 1), :], p3, 1.0, None, ALU.mult), m, name="rel%d" % b)
                        if squares:
                            ms = Ad(lambda e: e.activation(sq[:, b % 2, :].rearrange("p (a n) -> p a n", a=1), yt[:, bass.ds(n, 1), :],
                                                           ACT.Square), mx, "sqr%d" % (b % 2))
                            V(lambda e: e.tensor_tensor(acc[:], acc[:], sq[:, b % 2, :], ALU.add), ms, "accw", name="accw")
                            pr.name("sqr%d" % (b % 2), pr.names["accw"])
                    return go
                for j in range(2):
                    panel(ksrc(w, k0, i * 512 + j * 256), [tile_F(0, Yh, Yl, 2 * j, y_ready), tile_F(1, Yh, Yl, 2 * j + 1, y_ready)],
                          [epi(2 * j), epi(2 * j + 1)], more or j == 0)
            car = CARRY + ([("act", "sqr0", "sqr1"), ("dve", "accw")] if squares else [])
            if more:
                pr.loop(2, body, carry=car)
            else:
                body(0)
                body(1, False)
            if squares:
                pr.name("acc", pr.last("accw"))
            pr.name("y_free", now("pe"))

        def post(l, which, last=False, zero=False):
            m = rms_inverse(rms_sum(acc, psx[:, 3, :], "acc", "relx3", name="acc_read"), D, psx[:, 3, :])
            m = rms_spread(m, psx[:, 3, :])
            pr.wait("pool", now("act"))
            ms, mp = None, None
            for k in range(KD):
                t = tmp[:, k % 4, :]
                mt = V(lambda e: e.scalar_tensor_tensor(t, yt[:, k, :], GC[:, l, which, k:k + 1], psx[:, 3, :], ALU.mult, ALU.mult),
                       m, "tmp%d" % (k % 4))
                mx = (G if k % 2 else V)(lambda e: e.tensor_tensor(x[:, k, :], x[:, k, :], t, ALU.add), mt, name="tmp%d" % (k % 4))
                pr.name("xw%d" % k, mx)
                if zero:
                    pr.name("ytw", G(lambda e: e.memset(yt[:, k, :], 0.0), mt))
                if last:
                    continue
                ms = A(lambda e: e.activation(sq[:, k % 2, :], x[:, k, :], ACT.Square), mx, "sqr%d" % (k % 2))
                mp = square_sum(k, ms, "relx2")
            pr.name("relx3", mt)
            return mp

        def merged_gains():
            def mcol(l, c, who=0):
                o = 96 if who else 48 * l
                return mod[:, o + 8 * c:o + 8 * c + 8]
            for l in range(2):
                for w, name, c in ((0, "norm_mix_pre_2", 1), (1, "norm_mix_post_2", 2), (2, "norm_mlp_pre_2", 4), (3, "norm_mlp_post_2", 5)):
                    g = PK[:, col[name] + KD * l:col[name] + KD * l + KD]
                    V(lambda e: e.scalar_tensor_tensor(GC[:, l, w, :], mcol(l, c), 1.0 if w % 2 == 0 else 0.0, g, ALU.add, ALU.mult))
            g = PK[:, col["norm_mix_pre_2"]:col["norm_mix_pre_2"] + KD]
            V(lambda e: e.scalar_tensor_tensor(GC[:, 0, 4, :], mcol(0, 1, 1), 1.0, g, ALU.add, ALU.mult))
            m = V(lambda e: e.tensor_scalar(GC[:, 1, 4, 0:1], pc("attn_subln_2", 0), 1.0 - LAM_INIT, None, ALU.mult))
            pr.wait("dve", m)
            pr.wait("act", m)

        def shift(l, c, who=0):
            o = (96 if who else 48 * l) + 8 * c
            return lambda k: mod[:, o + k:o + k + 1]

        pr.dma_counter("ldd")

        def load_attention():
            for t in range(CT):
                pr.emit("act", lambda e: e.dma_start(QD[:, 2 * t:2 * t + 2, :].rearrange("p a n -> p (a n)"),
                                                     I["ctx_2"][0, t * P:(t + 1) * P, :]), ctr="ldd")
            pr.emit("act", lambda e: e.dma_start(ropeD[:], I["k_ropeD"]), ctr="ldd")
            ml = pr.emit("act", lambda e: e.dma_start(PD[:, 0, 0:256],
                                                      I["attn_lambda_2"][0].rearrange("a n -> (a n)").partition_broadcast(P)), ctr="ldd")
            pr.name("attention_in", ml)

        def attention2():
            win, wout = I["attn_w_qkv_2"][0], I["attn_w_out_2"][0]
            new_phase()
            ml = pr.last("attention_in")
            lamD = PD[:, 0, 0:256].rearrange("p (a n) -> p a n", a=4)
            norm(lambda k: GC[:, 0, 0, k:k + 1], shift(0, 0), free="h_free")
            pr.wait("dve", ml)
            m = V(lambda e: e.tensor_tensor_reduce(lamD[:, 0, :], lamD[:, 0, :], lamD[:, 1, :], 1.0, 0.0, ALU.mult, ALU.add, stD[:, 16:17]))
            m = V(lambda e: e.tensor_tensor_reduce(lamD[:, 2, :], lamD[:, 2, :], lamD[:, 3, :], 1.0, 0.0, ALU.mult, ALU.add, stD[:, 17:18]))
            m = A(lambda e: e.activation(stD[:, 18:20], stD[:, 16:18], ACT.Exp), m)
            nlam = stD[:, 20:21]
            m = V(lambda e: e.scalar_tensor_tensor(nlam, stD[:, 19:20], -LAM_INIT, stD[:, 18:19], ALU.add, ALU.subtract), m)
            for e in ("act", "dve"):
                pr.wait(e, "kst0", "kst1")
            pr.name("qk_free", now("dve"))
            p1D = rs[:].rearrange("p a n -> p (a n)")[:, 0:S + CTX]

            def body(i):
                def epi_lat(dst, b):
                    def go(m):
                        m = A(lambda e: e.activation(dst, ps[b][:], ACT.Copy), m, "qk_free", name="rel%d" % b)
                        rope(dst, ropeD, m)
                    return go

                def epi_ctx(dst, b):
                    def go(m):
                        V(lambda e: e.tensor_copy(dst, ps[b][:, 0:CTX]), m, "qk_free", name="rel%d" % b)
                    return go

                def epi_v(t0, c0, b):
                    def go(m):
                        V(lambda e: e.tensor_copy(VD[:, t0:t0 + 2, c0:c0 + 256], ps[b][:].rearrange("p (t n) -> p t n", t=2)),
                          m, "qk_free", name="rel%d" % b)
                    return go

                def u_ready(k):
                    return "u%d" % k
                for j in range(2):
                    panel(ksrc(win, 0, i * 512 + j * 256), [tile_F(0, Ah, Al, 2 * j, h_ready), tile_F(1, Ah, Al, 2 * j + 1, h_ready)],
                          [epi_lat(QD[:, 2 * j, :], 2 * j), epi_lat(QD[:, 2 * j + 1, :], 2 * j + 1)])
                for j in range(2):
                    h0, h1 = 2 * j, 2 * j + 1
                    panel(ksrc(win, 0, D + i * 512 + j * 256),
                          [tile_F(0, Ah, Al, 0), tile_F(0, Uh, Ul, 1, u_ready, cols=CTX), tile_F(1, Ah, Al, 2), tile_F(1, Uh, Ul, 3, cols=CTX)],
                          [epi_lat(KDt[:, h0, CTX:], 0), epi_ctx(KDt[:, h0, 0:CTX], 1), epi_lat(KDt[:, h1, CTX:], 2),
                           epi_ctx(KDt[:, h1, 0:CTX], 3)])
                for j in range(2):
                    panel(ksrc(win, 0, 2 * D + i * 512 + j * 256),
                          [tile_T((0, 1), Uh, Ul, 0), tile_T((0, 1), Ah, Al, 1), tile_T((2, 3), Ah, Al, 2)],
                          [epi_v(0, j * 256, 0), epi_v(2, j * 256, 1), epi_v(4, j * 256, 2)])
                qk_done = now("dve")
                NK = S + CTX

                def scores(h, j):
                    o = 8 * (j % 2)
                    out_m = []
                    for p in range(2):
                        pr.wait("pe", qk_done, "relx%d" % (2 * p), "relx%d" % (2 * p + 1))
                        q = QD[64 * p:64 * p + 64, h, j * P:(j + 1) * P]
                        c = 2 * p * S
                        pr.raw("pe", lambda e: e.matmul(psf[:, c:c + S], q, KDt[64 * p:64 * p + 64, h, 0:S], start=True, stop=True))
                        m = T(lambda e: e.matmul(psf[:, c + S:c + NK], q, KDt[64 * p:64 * p + 64, h, S:NK], start=True, stop=True))
                        m = V(lambda e: e.tensor_reduce(stD[:, o + p:o + p + 1], psf[:, c:c + NK], AX.X, ALU.max), m, "st%d" % (j % 2))
                        m = V(lambda e: e.tensor_scalar(stD[:, o + 2 + p:o + 3 + p], stD[:, o + p:o + p + 1], -0.125, None, ALU.mult), m)
                        dst, free = (p1D, "p1") if p else (PD[:, j % 2, :], "pd%d" % (j % 2))
                        m = A(lambda e: e.activation(dst, psf[:, c:c + NK], ACT.Exp, bias=stD[:, o + 2 + p:o + 3 + p], scale=0.125,
                                                     accum_out=stD[:, o + 4 + p:o + 5 + p]), m, free, name="relx%d" % (2 * p))
                        pr.name("relx%d" % (2 * p + 1), m)
                    m = V(lambda e: e.reciprocal(stD[:, o + 6:o + 8], stD[:, o + 4:o + 6]), m)
                    return V(lambda e: e.tensor_tensor(stD[:, o + 7:o + 8], stD[:, o + 7:o + 8], nlam, ALU.mult), m)

                def combine(h, j, m):
                    o = 8 * (j % 2)
                    m = V(lambda e: e.tensor_scalar(p1D, p1D, stD[:, o + 7:o + 8], None, ALU.mult), m)
                    a = PD[:, j % 2, :]
                    m = V(lambda e: e.scalar_tensor_tensor(a, a, stD[:, o + 6:o + 7], p1D, ALU.mult, ALU.add), m, name="p1")
                    pr.name("st%d" % (j % 2), m)
                    return m

                def flip(h, j, ma):
                    c = 2 * (j % 2)
                    pr.wait("pe", ma, "rel0")
                    for t in range(4):
                        m = T(lambda e: e.transpose(ps[0][:, t * P:(t + 1) * P], PD[:, j % 2, t * P:(t + 1) * P], ident[:]))
                    e0 = A(lambda e: e.activation(tmp[:, c, :], ps[0][:], ACT.Copy), m, "tmp%d" % c, name="rel0")
                    pr.wait("pe", "rel1")
                    for t in range(2):
                        m = T(lambda e: e.transpose(ps[1][:, t * P:(t + 1) * P], PD[:, j % 2, (4 + t) * P:(5 + t) * P], ident[:]))
                    pr.name("pd%d" % (j % 2), m)
                    e1 = V(lambda e: e.tensor_copy(tmp[:, c + 1, 0:256], ps[1][:, 0:256]), m, "tmp%d" % (c + 1), name="rel1")
                    return e0, e1

                def values(h, j, ev):
                    c, b = 2 * (j % 2), 2 + h % 2
                    pr.wait("pe", "rel%d" % b)
                    for t in range(6):
                        if t in (0, 4):
                            pr.wait("pe", ev[t // 4])
                        fn = lambda e: e.matmul(ps[b][:, j * P:(j + 1) * P], VD[:, t, h * P:(h + 1) * P],
                                                tmpf[:, c * S + t * P:c * S + (t + 1) * P], start=(t == 0), stop=(t == 5))
                        if t < 5:
                            pr.raw("pe", fn)
                        else:
                            m = T(fn, name="tmp%d" % c)
                    pr.name("tmp%d" % (c + 1), m)
                    if j < TT - 1:
                        return None
                    A(lambda e: e.activation(sq[:, 0, :], ps[b][:], ACT.Square), m, "sqr0")
                    ms = A(lambda e: e.activation(acc[:], ps[b][:], ACT.Copy), "acch")

                    def sums():
                        m = rms_inverse(rms_sum(sq[:, 0, :], ps[b], ms, name="sqr0"), P, ps[b])
                        return lambda: rest(m)

                    def rest(m):
                        m = rms_spread(m, ps[b])
                        m = V(lambda e: e.scalar_tensor_tensor(acc[:], acc[:], GC[:, 1, 4, 0:1], ps[b][:], ALU.mult, ALU.mult), m, name="rel%d" % b)
                        split_tile(acc[:], m, i * 4 + h, dyn=True, slot="acch")
                    return sums

                units = [(h, j) for h in range(4) for j in range(TT)]
                done = scores(*units[0])
                before, left = None, None
                for n in range(len(units) + 1):
                    ev = None
                    if n < len(units):
                        h, j = units[n]
                        ma = combine(h, j, done)
                        if n + 1 < len(units):
                            done = scores(*units[n + 1])
                        ev = flip(h, j, ma)
                    todo, left = left, None
                    if before:
                        left = values(*units[n - 1], before)
                    if todo:
                        left = todo() or left
                    before = ev
                while left:
                    left = left()
                pr.name("qk_free", now("pe"))
            pr.loop(2, body, carry=CARRY + [("act", "qk_free", "y_free", "tmp0", "tmp2", "sqr0", "sqr1", "acch", "p1", "pd0", "pd1"),
                                            ("dve", "qk_free", "y_free", "tmp1", "tmp3"),
                                            ("pe", "relx0", "relx1", "relx2", "relx3")])
            for k in range(KD):
                pr.name("y%d" % k, now("dve"))
            pr.name("h_free", now("pe"))
            pr.name("rsr0", pr.last("p1"))
            pr.name("rsr1", pr.last("p1"))
            new_phase()
            product_to_yt(wout, 0, squares=True)
            return post(0, 1, zero=True)

        def mlp(l, summed, last=False):
            norm(lambda k: GC[:, l, 2, k:k + 1], shift(l, 3), free="h_free", summed=summed)
            win, wout = I["w_mlp_in_2"][l], I["w_mlp_out_2"][l]

            def quarter(iq, more=True, squares=False):
                def inner(i):
                    def epi(b):
                        def go(m):
                            m = A(lambda e: e.activation(tmp[:, b, :], ps[b][:], ACT.Relu), m, "tmp%d" % b, name="rel%d" % b)
                            m = V(lambda e: e.tensor_tensor(tmp[:, b, :], tmp[:, b, :], tmp[:, b, :], ALU.mult), m)
                            pr.wait("act", "y_free")
                            pr.wait("dve", "y_free")
                            split_tile(tmp[:, b, :], m, i * 4 + b, dyn=True, slot="tmp%d" % b, name="yb%d" % b)
                        return go
                    for j in range(2):
                        panel(ksrc(win, 0, iq * D + i * 512 + j * 256), [tile_F(0, Ah, Al, 2 * j, h_ready), tile_F(1, Ah, Al, 2 * j + 1, h_ready)],
                              [epi(2 * j), epi(2 * j + 1)])
                pr.loop(2, inner, carry=CARRY + [("act", "tmp0", "tmp1", "tmp2", "tmp3")])
                if not pr.dry:
                    for b in range(4):
                        m = pr.names["yb%d" % b]
                        pr.names["y%d" % (4 + b)] = m
                        pr.names["y%d" % b] = Mark(m.ctr, m.const, m.levels, m.back + m.levels[-1].per[m.ctr])
                product_to_yt(wout, iq * KD, add=True, more=more, squares=squares)
            pr.loop(3, quarter, carry=CARRY + [("act", "tmp0", "tmp1", "tmp2", "tmp3", "y_free"), ("dve", "y_free")])
            quarter(3, more=not last, squares=True)
            pr.name("h_free", now("pe"))
            return post(l, 3, last)

        pr.dma_counter("ldf")
        pr.dma_counter("stf0")
        pr.dma_counter("stf1")
        TWO_PI = 2.0 * float(np.pi)
        C1 = 6.28125
        C2 = float(np.float32(TWO_PI - C1))
        C3 = float(np.float32(TWO_PI - C1 - C2))
        MAGIC = 1.5 * 2.0 ** 23
        PI_IN = float(np.nextafter(np.float32(np.pi), np.float32(0)))

        def load_filters():
            pr.wait("act", "h_free")
            ld = [(zF[:], I["k_z"]), (w1F[:], I["hy_filt_w1_2"][0]), (w2F[:], I["hy_filt_w2_2"][0].rearrange("a i j -> i a j")),
                  (woF[:], I["hy_filt_w_out_2"][0]), (colF[0:64, 0:1], I["hy_filt_b1_2"][0].rearrange("(p a) -> p a", a=1)),
                  (colF[0:64, 1:2], I["hy_filt_b2_2"][0, 0].rearrange("(p a) -> p a", a=1)),
                  (colF[0:64, 2:3], I["hy_filt_b2_2"][0, 1].rearrange("(p a) -> p a", a=1)),
                  (colF[0:64, 3:4], I["hy_filt_freq_2"][0].rearrange("(p a) -> p a", a=1)),
                  (colF[:, 4:9], I["k_tcol"]), (dlF[:], I["k_delta"].partition_broadcast(P)),
                  (tabF[:, 0, :, :], I["k_tab0"][0].rearrange("(k p) n -> p k n", p=P)),
                  (tabF[:, 1, :, :], I["k_tab0"][1].rearrange("(k p) n -> p k n", p=P))]
            for d, s_ in ld:
                ml = pr.emit("act", lambda e: e.dma_start(d, s_), ctr="ldf")
            pr.name("filters_in", ml)

        def context_tiles(ks):
            cst = QD[:].rearrange("p (t a) n -> p t (a n)", t=CT)
            pr.wait("pe", "attention_in")
            for k in ks:
                b = k % 2
                pr.wait("pe", "rel%d" % b)
                for t in range(CT):
                    m = T(lambda e: e.transpose(ps[b][:, t * P:(t + 1) * P], cst[:, t, k * P:(k + 1) * P], ident[:]))
                m = V(lambda e: e.tensor_copy(xctx[:, k, :], ps[b][:, 0:CTX]), m, name="rel%d" % b)
                ms = A(lambda e: e.activation(sq[:, b, 0:CTX], xctx[:, k, :], ACT.Square), m, "sqr%d" % b)
                m = square_sum(k, ms, "relx2", cols=CTX)
            return m

        def filters():
            new_phase()
            load_attention()
            merged_gains()
            for e in ("pe", "dve", "act"):
                pr.wait(e, "filters_in")
            m = None
            for j in range(3):
                lhs, rhs = (w1F[:], zF[:]) if j == 0 else (w2F[:, j - 1, :], hdF[:, (j - 1) % 2, :])
                pr.wait("pe", "relx0")
                m = T(lambda e: e.matmul(psx[0:64, 0, :], lhs, rhs, start=True, stop=True), *([m] if m else []))
                a, k = tmp[0:64, 0, :], kF[:]
                m = V(lambda e: e.tensor_scalar(a, psx[0:64, 0, :], colF[0:64, j:j + 1], colF[0:64, 3:4], ALU.add, ALU.mult), m, name="relx0")
                m = V(lambda e: e.tensor_scalar(k, a, 1.0 / TWO_PI, MAGIC, ALU.mult, ALU.add), m)
                m = V(lambda e: e.tensor_scalar(k, k, MAGIC, None, ALU.subtract), m)
                for c in (C1, C2, C3):
                    m = V(lambda e: e.scalar_tensor_tensor(a, k, -c, a, ALU.mult, ALU.add), m)
                m = V(lambda e: e.tensor_scalar(a, a, -PI_IN, PI_IN, ALU.max, ALU.min), m)
                m = A(lambda e: e.activation(hdF[:, j % 2, :], a, ACT.Sin), m, name="tmp0")
                summed = context_tiles(range(3 * j, min(3 * j + 3, KD)))
            hd = hdF[:, 0, :]
            norm(lambda k: GC[:, 0, 4, k:k + 1], shift(0, 0, 1), xctx, Uh, Ul, free="relx3", cols=CTX, tag="u", summed=summed)
            for e in ("act", "dve"):
                pr.wait(e, now("norm_act"), now("norm_dve"), now("norm_pool"))
            for half in range(2):
                c0 = half * 512
                for t in range(TT):
                    pr.wait("pe", m, "relx0", "relx1")
                    pr.raw("pe", lambda e: e.matmul(psx[:, 0, :], hd[:, t * P:(t + 1) * P], woF[:, c0:c0 + 512], start=True, stop=True))
                    mp = T(lambda e: e.matmul(psx[:, 1, :], hd[:, t * P:(t + 1) * P], woF[:, D + c0:D + c0 + 512], start=True, stop=True))
                    md = A(lambda e: e.activation(tmp[:, 0, :], dlF[:, c0:c0 + 512], ACT.Exp, scale=colF[:, 4 + t:5 + t]), now("dve"), now("act"))
                    m1 = V(lambda e: e.tensor_tensor(tmp[:, 1, :], psx[:, 0, :], tmp[:, 0, :], ALU.mult), mp, md, now("dve"), "hs_free", name="relx0")
                    if t == 0:
                        m2 = V(lambda e: e.scalar_tensor_tensor(tmp[:, 2, :], psx[:, 1, :], colF[:, 8:9], tmp[:, 0, :], ALU.mult, ALU.mult), name="relx1")
                    else:
                        m2 = V(lambda e: e.tensor_tensor(tmp[:, 2, :], psx[:, 1, :], tmp[:, 0, :], ALU.mult), name="relx1")
                    V(lambda e: e.tensor_tensor(hsF[:, t, :], tmp[:, 1, :], tmp[:, 2, :], ALU.add), m2)
                    mh = V(lambda e: e.tensor_tensor(hdiffF[:, t, :], tmp[:, 1, :], tmp[:, 2, :], ALU.subtract), m2)
                for fi in range(TT):
                    for w, src in ((0, hsF), (1, hdiffF)):
                        pr.wait("pe", mh, "relx%d" % (2 + w))
                        for k in range(TT):
                            fn = lambda e: e.matmul(psx[:, 2 + w, :], tabF[:, w, k, fi * P:(fi + 1) * P], src[:, k, :], start=(k == 0), stop=(k == TT - 1))
                            if k < TT - 1:
                                pr.raw("pe", fn)
                            else:
                                m3 = T(fn)
                        mk = A(lambda e: e.activation(kcF[:, w, :], psx[:, 2 + w, :], ACT.Copy, scale=1.0 / S), m3, "kst%d" % w, name="relx%d" % (2 + w))
                        pr.wait("act", mk)
                        pr.emit("act", lambda e: e.dma_start(kspec[w, fi, :, c0:c0 + 512], kcF[:, w, :]), ctr="stf%d" % w, name="kst%d" % w)
                pr.name("hs_free", now("pe"))
            pr.name("tmp0", now("dve"))

        pr.dma_counter("ldh")
        pr.dma_counter("ldk")

        def hyena(summed):
            win, wout = I["hy_w_in_2"][0], I["hy_w_out_2"][0]
            new_phase()
            for r in range(2):
                V(lambda e: e.memset(uH[:, r, 0:1], 0.0))
                mz = V(lambda e: e.memset(uH[:, r, S + 1:S + 2], 0.0))
            pr.wait("act", "kst0", "kst1")
            for w in range(2):
                pr.emit("act", lambda e: e.dma_start(tabH[:, w, :, :], I["k_tabs"][w].rearrange("(k p) n -> p k n", p=P)), ctr="ldh")
            for w in range(2):
                m_k0 = pr.emit("act", lambda e: e.dma_start(kS0[:, w, :, :], kspec[w, :, :, 0:512].rearrange("f p n -> p f n")), ctr="ldh")
            norm(lambda k: GC[:, 1, 0, k:k + 1], shift(1, 0), free="h_free", summed=summed)
            pr.wait("dve", mz)

            def body(i):
                for jj in range(2):
                    def epi(part, f, b):
                        def go(m):
                            n = i * 4 + jj * 2 + f
                            r = b % 2
                            pcol = lambda name, o: PK[:, bass.ds(col[name] + o + n, 1)]
                            m = Ad(lambda e: e.activation(uH[:, r, 1:S + 1], ps[b][:], ACT.Identity, bias=pcol("hy_b_in_2", part * KD)),
                                   m, "uhr%d" % r, name="rel%d" % b)
                            t = tmp[:, f if part == 1 else 2 + f, :]
                            tn = "tmp%d" % (f if part == 1 else 2 + f)
                            taps = [pcol("hy_w_short_2", tap * 3 * KD + part * KD) for tap in range(3)]
                            m = V(lambda e: e.tensor_scalar(t, uH[:, r, 1:S + 1], taps[1], pcol("hy_b_short_2", part * KD), ALU.mult, ALU.add), m, tn)
                            m = V(lambda e: e.scalar_tensor_tensor(t, uH[:, r, 0:S], taps[0], t, ALU.mult, ALU.add), m)
                            last = t if part else x0H[:, bass.ds(n, 1), :].rearrange("p a n -> p (a n)")
                            m = V(lambda e: e.scalar_tensor_tensor(last, uH[:, r, 2:S + 2], taps[2], t, ALU.mult, ALU.add), m, name="uhr%d" % r)
                            if part == 0:
                                pr.name(tn, m)
                            if part == 2:
                                m = V(lambda e: e.tensor_tensor(wH[:, bass.ds(n, 1), :].rearrange("p a n -> p (a n)"), tmp[:, f, :], t, ALU.mult),
                                      m, name="tmp%d" % f)
                                pr.name("tmp%d" % (2 + f), m)
                        return go
                    for part in range(3):
                        b = 2 * ((jj * 3 + part) % 2)
                        panel(ksrc(win, 0, part * D + i * 512 + jj * 256), [tile_F(0, Ah, Al, b, h_ready), tile_F(1, Ah, Al, b + 1, h_ready)],
                              [epi(part, 0, b), epi(part, 1, b + 1)])
            pr.loop(2, body, carry=CARRY + [("act", "uhr0", "uhr1"), ("dve", "tmp0", "tmp1", "tmp2", "tmp3")])
            pr.name("h_free", now("pe"))
            new_phase()
            for w in range(2):
                m_k1 = pr.emit("act", lambda e: e.dma_start(kS[:, w, :, :], kspec[w, :, :, 512:1024].rearrange("f p n -> p f n")), ctr="ldk")
            for half, (spectra, m_k) in enumerate(((kS0, m_k0), (kS, m_k1))):
                for k in range(TT):
                    b = k % 4
                    pr.wait("pe", "rel%d" % b)
                    for t in range(TT):
                        m = T(lambda e: e.transpose(ps[b][:, t * P:(t + 1) * P], wH[:, 4 * half + k, t * P:(t + 1) * P], ident[:]))
                    m = V(lambda e: e.tensor_copy(wtH[:, :, k * P:(k + 1) * P], ps[b][:].rearrange("p (t n) -> p t n", t=TT)), m, "wt_free", name="rel%d" % b)
                pr.wait("pe", m, m_k)
                pr.wait("dve", m_k)
                for fi in range(TT):
                    bc, bs = 2 * (fi % 2), 2 * (fi % 2) + 1
                    for w, b in ((0, bc), (1, bs)):
                        pr.wait("pe", "rel%d" % b)
                        for k in range(TT):
                            fn = lambda e: e.matmul(ps[b][:], tabH[:, w, k, fi * P:(fi + 1) * P], wtH[:, k, :], start=(k == 0), stop=(k == TT - 1))
                            if k < TT - 1:
                                pr.raw("pe", fn)
                            else:
                                m = T(fn)
                    yr, yi, kc, ks = yS[:, 0, fi, :], yS[:, 1, fi, :], spectra[:, 0, fi, :], spectra[:, 1, fi, :]
                    V(lambda e: e.tensor_tensor(yr, ps[bc][:], kc, ALU.mult), m, "ys_free")
                    a = V(lambda e: e.tensor_tensor(tmp[:, 0, :], ps[bs][:], ks, ALU.mult), "tmp0")
                    V(lambda e: e.tensor_tensor(yi, ps[bc][:], ks, ALU.mult), name="rel%d" % bc)
                    b2 = V(lambda e: e.tensor_tensor(tmp[:, 1, :], ps[bs][:], kc, ALU.mult), "tmp1", name="rel%d" % bs)
                    V(lambda e: e.tensor_tensor(yr, yr, tmp[:, 0, :], ALU.subtract), a, name="tmp0")
                    my = V(lambda e: e.tensor_tensor(yi, yi, tmp[:, 1, :], ALU.add), b2, name="tmp1")
                pr.name("wt_free", now("pe"))
                for n in range(4):
                    g = 4 * half + n
                    b = n
                    pr.wait("pe", my, "rel%d" % b)
                    for w in range(2):
                        for fi in range(TT):
                            fn = lambda e: e.matmul(ps[b][:], yS[:, w, fi, n * P:(n + 1) * P], tabH[:, w, fi, :], start=(w + fi == 0), stop=(w == 1 and fi == TT - 1))
                            if w == 0 or fi < TT - 1:
                                pr.raw("pe", fn)
                            else:
                                m = T(fn)
                    t = tmp[:, 2 + n % 2, :]
                    tn = "tmp%d" % (2 + n % 2)
                    m = V(lambda e: e.scalar_tensor_tensor(t, wH[:, g, :], pc("hy_bias_2", g), ps[b][:], ALU.mult, ALU.add), m, tn, name="rel%d" % b)
                    m = V(lambda e: e.tensor_tensor(t, t, x0H[:, g, :], ALU.mult), m)
                    split_tile(t, m, g, slot=tn, name="y%d" % g)
                pr.name("ys_free", now("pe"))
            new_phase()
            product_to_yt(wout, 0, bias="hy_b_out_2", squares=True)
            return post(1, 1, zero=True)

        mixer_a(0, 0, summed0)
        mixer_b()
        mixer_c()
        mixer_a(3, 1, load_ahead=load_filters)
        filters()
        summed = attention2()
        summed = mlp(0, summed)
        summed = hyena(summed)
        mlp(1, summed, last=True)
        new_phase()
        pr.dma_counter("out")
        for t in range(TT):
            for q in range(2):
                b = (2 * t + q) % 4
                pr.wait("pe", "rel%d" % b)
                for k in range(4):
                    m = T(lambda e: e.transpose(ps[b][:, k * P:(k + 1) * P], x[:, 4 * q + k, t * P:(t + 1) * P], ident[:]))
                m = V(lambda e: e.tensor_copy(stage[:, t, q * 512:(q + 1) * 512], ps[b][:]), m, name="rel%d" % b)
            pr.wait("act", m)
            mo = pr.emit("act", lambda e: e.dma_start(out[0, t * P:(t + 1) * P, :], stage[:, t, :]), ctr="out")
        pr.wait("act", mo, "kst0", "kst1")
        pr.put_waits("act")


_INS = ["x", "norm_gain", "a_w_in", "a_v_gain", "a_w_s", "a_b_s", "a_w_out", "b_w_in", "b_q_gain", "b_k_gain", "b_w_out",
        "c_w_in", "c_w_grp", "c_scale", "c_w_out", "c_2", "ctx_2", "c_ctx_2", "w_mod_2", "b_mod_2", "norm_mix_pre_2",
        "norm_mix_post_2", "norm_mlp_pre_2", "norm_mlp_post_2", "w_mlp_in_2", "w_mlp_out_2", "attn_w_qkv_2", "attn_w_out_2",
        "attn_lambda_2", "attn_subln_2", "hy_w_in_2", "hy_b_in_2", "hy_w_short_2", "hy_b_short_2", "hy_filt_w1_2",
        "hy_filt_b1_2", "hy_filt_w2_2", "hy_filt_b2_2", "hy_filt_freq_2", "hy_filt_w_out_2", "hy_bias_2", "hy_w_out_2",
        "hy_b_out_2"]


def shape_constants():
    f = np.float32
    c = {"k_ident": np.eye(P, dtype=f)}
    def rope(freq_rows, pos):
        ang = (pos[None, :].astype(f) * freq_rows[:, None].astype(f)).astype(f)
        return np.cos(ang).astype(f), np.sin(ang).astype(f)
    inv = np.power(f(500000.0), -np.arange(16, dtype=f) / f(16)).astype(f)
    pos = np.arange(S, dtype=f)
    co, si = rope(inv, pos)
    c["k_ropeB"] = np.stack([np.concatenate([co, co]), np.concatenate([-si, si])], axis=1)
    inv = (f(10000.0) ** (-np.arange(16, dtype=f) / f(16))).astype(f)
    blocks = []
    for p in (np.repeat(np.arange(S // 64), 64), np.tile(np.arange(64), S // 64)):
        co, si = rope(inv, p)
        blocks.append(np.stack([np.concatenate([co, co]), np.concatenate([-si, si])], axis=1))
    c["k_ropeD"] = np.concatenate(blocks * 2, axis=0)
    out = []
    q = np.arange(P)[:, None]
    for j in range(TT):
        for g, (span, dil) in enumerate(((128, 1), (512, 4), (2048, 16))):
            for t in range(max(0, j - 1) if g == 0 else 0, j + 1):
                d = (j * P + q) - (t * P + np.arange(P)[None, :])
                out.append(np.where((d >= 0) & (d <= span) & (d % dil == 0), 0.0, NEG))
    c["k_maskB"] = np.concatenate(out, axis=1)
    c["k_cnt"] = np.stack([1.0 / np.minimum(np.arange(S) + 1, w) for w in (2, 4, 8, 16)])
    t = np.linspace(0.0, 1.0, S, dtype=f)[:, None]
    w = (2.0 * np.pi * np.arange(S, dtype=f)[:, None] / S).astype(f)
    fr = np.linspace(1e-4, 15, 16, dtype=f)[None, :]
    c["k_z"] = np.concatenate([t, np.cos(fr * w), -np.sin(fr * w)], axis=-1).T
    tc = np.zeros((P, 5))
    tc[:, 0:4] = -t.reshape(TT, P).T
    tc[1:, 4] = 1.0
    c["k_tcol"] = tc
    c["k_delta"] = np.abs(np.linspace(np.log(1e-2) / 1.5, np.log(1e-2) / 0.3, D, dtype=f))
    fq = (np.arange(S) + 0.5)
    a = 2 * np.pi * np.outer(np.arange(S), fq) / (2 * S)
    c["k_tab0"] = np.stack([np.cos(a), np.sin(a)])
    a = 2 * np.pi * np.outer(np.arange(S) + 0.5, fq) / (2 * S)
    c["k_tabs"] = np.stack([np.cos(a), np.sin(a)])
    return {n: np.ascontiguousarray(v.astype(f)) for n, v in c.items()}


def kernel(**inputs):
    import concourse.bacc as _bacc
    from concourse.bass_utils import run_bass_kernel_spmd as _run

    nc = _bacc.Bacc("TRN2", target_bir_lowering=False, num_devices=1)
    arrays, aps = {}, {}
    given = {n: np.ascontiguousarray(inputs[n]) for n in _INS}
    given.update(shape_constants())
    for name, a in given.items():
        arrays[f"in_{name}_dram"] = a
        aps[name] = nc.dram_tensor(f"in_{name}_dram", a.shape, mybir.dt.from_np(a.dtype), kind="ExternalInput").ap()
    out = nc.dram_tensor("out_0_dram", (1, S, D), F32, kind="ExternalOutput").ap()
    build(nc, aps, out)
    r = _run(nc, [arrays], core_ids=[0])
    return r.results[0]["out_0_dram"]
```
